# Optimizing a Trainium2 kernel written in Bass

```python
import math
import jax
import jax.numpy as jnp
from jax import lax
import numpy as np

D_MODEL = 1024
BATCH = 1
SEQ = 512
DEPTH = 2

GRID_W = 64
CTX_LEN = 256
F32 = jnp.float32
EPS = 1e-6
NEG = -1e30
N_MOD = 9
FFN_RESIDUAL = 0.5
D_FF = 256 * math.ceil(8 * D_MODEL / 3 / 256)
HEAD_DIM = 64
A_Q_HEADS = D_MODEL // (2 * HEAD_DIM)
A_KV_HEADS = max(1, A_Q_HEADS // 4)
WINDOW = 128
BLOCK = 128
ROPE_BASE = 10000.0
R_DIM = 64
R_HEADS = D_MODEL // (2 * R_DIM)
R_CHUNK = 128
R_MIN_EXP = 5.0
A_Q_W = A_Q_HEADS * HEAD_DIM
A_KV_W = A_KV_HEADS * HEAD_DIM
R_W = R_HEADS * R_DIM
Q_WIDTHS = (A_Q_W, R_W, R_W)
KV_WIDTHS = (A_KV_W, A_KV_W, R_W, R_W)
Q_SIDE = sum(Q_WIDTHS)
IN_W = Q_SIDE + sum(KV_WIDTHS)
MIX_W = A_Q_W + R_W
HY_EMB = 33
HY_ORDER = 64
HY_SHORT = 3
HY_MAX_DECAY = math.log(1e-2) / 0.3
HY_MIN_DECAY = math.log(1e-2) / 1.5
N_EVEN = (DEPTH + 1) // 2
N_ODD = DEPTH // 2

kernel_name = 'hybrid_swa_retention_hyena_prefix_dit'

def rmsnorm(x, g):
    xf = x.astype(F32)
    y = xf * lax.rsqrt(jnp.mean(xf * xf, -1, keepdims=True) + EPS)
    return (y * g.astype(F32)).astype(x.dtype)

def adaln_in(x, g, m, i):
    return rmsnorm(x, g) * (1.0 + m[:, :, 3 * i + 1]) + m[:, :, 3 * i]

def adaln_out(x, y, g, m, i, w):
    return x + w * m[:, :, 3 * i + 2] * rmsnorm(y, g)

def swiglu(h, w_gate, w_up, w_down):
    return (jax.nn.silu(h @ w_gate) * (h @ w_up)) @ w_down

def macaron_half(s, m, i, g_pre, g_post, w_gate, w_up, w_down):
    h = adaln_in(s, g_pre, m, i)
    return adaln_out(s, swiglu(h, w_gate, w_up, w_down), g_post, m, i, FFN_RESIDUAL)

def split_cols(z, widths):
    idx = np.cumsum(widths)[:-1].tolist()
    return jnp.split(z, idx, axis=-1)

def heads(a, d):
    return a.reshape(a.shape[0], a.shape[1], -1, d)

def axial_rope(L):
    n_rows = L // GRID_W
    row = jnp.repeat(jnp.arange(n_rows, dtype=F32), GRID_W)
    col = jnp.tile(jnp.arange(GRID_W, dtype=F32), n_rows)
    nf = HEAD_DIM // 4
    inv = ROPE_BASE ** (-jnp.arange(nf, dtype=F32) / nf)
    ang = jnp.concatenate([row[:, None] * inv, col[:, None] * inv], -1)
    return jnp.cos(ang), jnp.sin(ang)

def line_rope(L, d):
    inv = ROPE_BASE ** (-jnp.linspace(0.0, 1.0, d // 2, dtype=F32))
    ang = jnp.arange(L, dtype=F32)[:, None] * inv
    return jnp.cos(ang), jnp.sin(ang)

def apply_rope(x, cos, sin):
    half = x.shape[-1] // 2
    x1, x2 = x[..., :half], x[..., half:]
    c, s = cos[None, :, None], sin[None, :, None]
    return jnp.concatenate([x1 * c - x2 * s, x1 * s + x2 * c], -1).astype(x.dtype)

def window_attention(q, k, v, kc, vc, sink):
    Bn, L, Hq, dh = q.shape
    G = k.shape[2]
    R = Hq // G
    nb = L // BLOCK
    T = BLOCK
    qb = q.reshape(Bn, nb, T, G, R, dh)
    pad = ((0, 0), (T, T), (0, 0), (0, 0))
    kp = jnp.pad(k, pad).reshape(Bn, nb + 2, T, G, dh)
    vp = jnp.pad(v, pad).reshape(Bn, nb + 2, T, G, dh)
    kb = jnp.concatenate([kp[:, :-2], kp[:, 1:-1], kp[:, 2:]], axis=2)
    vb = jnp.concatenate([vp[:, :-2], vp[:, 1:-1], vp[:, 2:]], axis=2)
    qi = jnp.arange(T)[:, None]
    kj = jnp.arange(3 * T)[None, :]
    kpos = jnp.arange(nb)[:, None, None] * T - T + kj
    valid = (jnp.abs(kj - T - qi) <= WINDOW)[None] & (kpos >= 0) & (kpos < L)
    scale = HEAD_DIM ** -0.5
    s_loc = jnp.einsum('bnqgrd,bnkgd->bngrqk', qb, kb).astype(F32) * scale
    s_loc = jnp.where(valid[None, :, None, None], s_loc, NEG)
    s_ctx = jnp.einsum('bnqgrd,bcgd->bngrqc', qb, kc).astype(F32) * scale
    s_sink = jnp.broadcast_to(sink.astype(F32).reshape(G, R)[None, None, :, :, None, None],
                              s_loc.shape[:-1] + (1,))
    p = jax.nn.softmax(jnp.concatenate([s_loc, s_ctx, s_sink], -1), axis=-1).astype(v.dtype)
    o = (jnp.einsum('bngrqk,bnkgd->bnqgrd', p[..., :3 * T], vb)
         + jnp.einsum('bngrqc,bcgd->bnqgrd', p[..., 3 * T:-1], vc))
    return o.reshape(Bn, L, Hq * dh)

def context_attention(qc, kc, vc, sink):
    Bn, C, Hq, dh = qc.shape
    G = kc.shape[2]
    R = Hq // G
    qg = qc.reshape(Bn, C, G, R, dh)
    s = jnp.einsum('bqgrd,bkgd->bgrqk', qg, kc).astype(F32) * HEAD_DIM ** -0.5
    s_sink = jnp.broadcast_to(sink.astype(F32).reshape(G, R)[None, :, :, None, None], s.shape[:-1] + (1,))
    p = jax.nn.softmax(jnp.concatenate([s, s_sink], -1), axis=-1)[..., :-1].astype(vc.dtype)
    return jnp.einsum('bgrqk,bkgd->bqgrd', p, vc).reshape(Bn, C, Hq * dh)

def retention_chunks(q, k, v, log_g, s0):
    Bn, L, H, _ = q.shape
    dv = v.shape[-1]
    n = L // R_CHUNK
    T = R_CHUNK
    idx = jnp.arange(T, dtype=F32)
    diff = idx[:, None] - idx[None, :]
    d_in = jnp.where(diff[None] >= 0, jnp.exp(jnp.maximum(diff, 0.0)[None] * log_g[:, None, None]), 0.0)
    d_q = jnp.exp((idx + 1.0)[None, :] * log_g[:, None])
    d_k = jnp.exp((T - 1.0 - idx)[None, :] * log_g[:, None])
    d_c = jnp.exp(T * log_g)

    def to_chunks(a):
        return a.astype(F32).reshape(Bn, n, T, H, -1).transpose(1, 0, 3, 2, 4)

    def step(S, inp):
        qi, ki, vi = inp
        att = jnp.einsum('bhtd,bhsd->bhts', qi, ki) * d_in
        o = (jnp.einsum('bhts,bhse->bhte', att, vi)
             + jnp.einsum('bhtd,bhde->bhte', qi, S) * d_q[None, :, :, None])
        S = S * d_c[None, :, None, None] + jnp.einsum('bhsd,bhse->bhde', ki * d_k[None, :, :, None], vi)
        return S, o

    S, o = lax.scan(step, s0, (to_chunks(q), to_chunks(k), to_chunks(v)))
    return o.transpose(1, 0, 3, 2, 4).reshape(Bn, L, H, dv), S

def retention_final_state(k, v, log_g):
    L = k.shape[1]
    w = jnp.exp((L - 1.0 - jnp.arange(L, dtype=F32))[:, None] * log_g[None, :])
    return jnp.einsum('bthd,bthe,th->bhde', k.astype(F32), v.astype(F32), w)

def retention_out(o, g):
    o = o * lax.rsqrt(jnp.mean(o * o, -1, keepdims=True) + EPS)
    return o.reshape(o.shape[0], o.shape[1], -1).astype(g.dtype) * jax.nn.silu(g)

def even_mixer(h, hc, w_in, sink, decay_logit, w_out, rope_a, rope_r, ctx_full):
    lg_f = jax.nn.log_sigmoid(decay_logit[0].astype(F32))
    lg_b = jax.nn.log_sigmoid(decay_logit[1].astype(F32))
    z = h @ w_in
    aq, rq, rg = split_cols(z[..., :Q_SIDE], Q_WIDTHS)
    ak, av, rk, rv = split_cols(z[..., Q_SIDE:], KV_WIDTHS)
    aq = apply_rope(heads(aq, HEAD_DIM), *rope_a)
    ak = apply_rope(heads(ak, HEAD_DIM), *rope_a)
    av = heads(av, HEAD_DIM)
    rq = apply_rope(heads(rq, R_DIM), *rope_r)
    rk = apply_rope(heads(rk, R_DIM), *rope_r) * R_DIM ** -0.5
    rv = heads(rv, R_DIM)
    if ctx_full:
        zc = hc @ w_in
        aqc, rqc, rgc = split_cols(zc[..., :Q_SIDE], Q_WIDTHS)
        akc, avc, rkc, rvc = split_cols(zc[..., Q_SIDE:], KV_WIDTHS)
    else:
        akc, avc, rkc, rvc = split_cols(hc @ w_in[:, Q_SIDE:], KV_WIDTHS)
    akc, avc = heads(akc, HEAD_DIM), heads(avc, HEAD_DIM)
    rkc, rvc = heads(rkc, R_DIM) * R_DIM ** -0.5, heads(rvc, R_DIM)
    if ctx_full:
        aqc, rqc = heads(aqc, HEAD_DIM), heads(rqc, R_DIM)
        zero = jnp.zeros((hc.shape[0], R_HEADS, R_DIM, R_DIM), F32)
        oc_f, s_f = retention_chunks(rqc, rkc, rvc, lg_f, zero)
        oc_b, s_b = retention_chunks(rqc[:, ::-1], rkc[:, ::-1], rvc[:, ::-1], lg_b, zero)
        yc = jnp.concatenate([context_attention(aqc, akc, avc, sink),
                              retention_out(oc_f + oc_b[:, ::-1], rgc)], -1) @ w_out
    else:
        s_f = retention_final_state(rkc, rvc, lg_f)
        s_b = retention_final_state(rkc[:, ::-1], rvc[:, ::-1], lg_b)
        yc = None
    o_f, _ = retention_chunks(rq, rk, rv, lg_f, s_f)
    o_b, _ = retention_chunks(rq[:, ::-1], rk[:, ::-1], rv[:, ::-1], lg_b, s_b)
    a = window_attention(aq, ak, av, akc, avc, sink)
    y = jnp.concatenate([a, retention_out(o_f + o_b[:, ::-1], rg)], -1) @ w_out
    return y, yc

def hyena_filter(L, f0, fb0, f1, fb1, f2, fb2, f3, freq):
    t = jnp.linspace(0.0, 1.0, L, dtype=F32)[:, None]
    bands = (HY_EMB - 1) // 2
    w = 2.0 * math.pi * jnp.arange(L, dtype=F32)[:, None] / L
    f = jnp.linspace(1e-4, bands - 1, bands, dtype=F32)[None]
    z = jnp.concatenate([t, jnp.cos(f * w), -jnp.sin(f * w)], -1)
    fr = freq.astype(F32)
    a = jnp.sin(fr * (z @ f0.astype(F32) + fb0.astype(F32)))
    a = jnp.sin(fr * (a @ f1.astype(F32) + fb1.astype(F32)))
    a = jnp.sin(fr * (a @ f2.astype(F32) + fb2.astype(F32)))
    k = (a @ f3.astype(F32)).reshape(L, 2, D_MODEL)
    deltas = jnp.abs(jnp.linspace(HY_MIN_DECAY, HY_MAX_DECAY, D_MODEL, dtype=F32))
    k = k * jnp.exp(-t * deltas)[:, None, :]
    return k[:, 0], k[:, 1]

def bidir_fftconv(u, k_f, k_b, bias):
    L = u.shape[1]
    k = jnp.concatenate([k_f, jnp.zeros_like(k_f[:1]), k_b[:0:-1]], 0)
    uf = jnp.fft.rfft(u.astype(F32), n=2 * L, axis=1)
    kf = jnp.fft.rfft(k, n=2 * L, axis=0)
    y = jnp.fft.irfft(uf * kf[None], n=2 * L, axis=1)[:, :L]
    return (y + u.astype(F32) * bias.astype(F32)).astype(u.dtype)

def short_conv(z, w, b):
    L = z.shape[1]
    half = HY_SHORT // 2
    zp = jnp.pad(z, ((0, 0), (half, half), (0, 0)))
    return sum(zp[:, i:i + L] * w[i] for i in range(HY_SHORT)) + b

def hyena_mixer(h, w_in, b_in, w_sh, b_sh, f0, fb0, f1, fb1, f2, fb2, f3, freq, bias, w_out):
    L = h.shape[1]
    z = short_conv(h @ w_in + b_in, w_sh, b_sh)
    x0, x1, v = jnp.split(z, 3, axis=-1)
    k_f, k_b = hyena_filter(L, f0, fb0, f1, fb1, f2, fb2, f3, freq)
    y = x0 * bidir_fftconv(v * x1, k_f, k_b, bias)
    return y @ w_out

def setup_inputs(seed: int = 0) -> dict:
    key = jax.random.key(seed)
    ks = iter(jax.random.split(key, 32))
    D = D_MODEL

    def nrm(shape, s):
        return jax.random.normal(next(ks), shape, F32) * s

    expo = jnp.arange(R_HEADS, dtype=F32) + R_MIN_EXP
    decay0 = jnp.log(2.0 ** expo - 1.0)
    return {
        'x': nrm((BATCH, SEQ, D), 1.0),
        'c': nrm((BATCH, D), 1.0),
        'ctx': nrm((BATCH, CTX_LEN, D), 1.0),
        'c_ctx': nrm((D,), 1.0),
        'w_mod': nrm((DEPTH, D, N_MOD * D), 0.5 * D ** -0.5),
        'b_mod': nrm((DEPTH, N_MOD * D), 0.02),
        'norm_pre': 1.0 + nrm((DEPTH, 3, D), 0.02),
        'norm_post': 1.0 + nrm((DEPTH, 3, D), 0.02),
        'ffn_gate': nrm((DEPTH, 2, D, D_FF), D ** -0.5),
        'ffn_up': nrm((DEPTH, 2, D, D_FF), D ** -0.5),
        'ffn_down': nrm((DEPTH, 2, D_FF, D), D_FF ** -0.5),
        'mix_w_in': nrm((N_EVEN, D, IN_W), D ** -0.5),
        'attn_sink': nrm((N_EVEN, A_Q_HEADS), 0.5),
        'ret_decay': decay0 + nrm((N_EVEN, 2, R_HEADS), 0.1),
        'mix_w_out': nrm((N_EVEN, MIX_W, D), MIX_W ** -0.5),
        'hy_w_in': nrm((N_ODD, D, 3 * D), D ** -0.5),
        'hy_b_in': nrm((N_ODD, 3 * D), 0.02),
        'hy_short_w': nrm((N_ODD, HY_SHORT, 3 * D), HY_SHORT ** -0.5),
        'hy_short_b': nrm((N_ODD, 3 * D), 0.02),
        'hy_f0': nrm((N_ODD, HY_EMB, HY_ORDER), HY_EMB ** -0.5),
        'hy_fb0': nrm((N_ODD, HY_ORDER), 0.1),
        'hy_f1': nrm((N_ODD, HY_ORDER, HY_ORDER), HY_ORDER ** -0.5),
        'hy_fb1': nrm((N_ODD, HY_ORDER), 0.1),
        'hy_f2': nrm((N_ODD, HY_ORDER, HY_ORDER), HY_ORDER ** -0.5),
        'hy_fb2': nrm((N_ODD, HY_ORDER), 0.1),
        'hy_f3': nrm((N_ODD, HY_ORDER, 2 * D), 0.05 * HY_ORDER ** -0.5),
        'hy_freq': 1.0 + nrm((N_ODD, HY_ORDER), 0.02),
        'hy_bias': nrm((N_ODD, D), 1.0),
        'hy_w_out': nrm((N_ODD, D, D), D ** -0.5),
    }

def reference(x, c, ctx, c_ctx, w_mod, b_mod, norm_pre, norm_post, ffn_gate, ffn_up, ffn_down,
              mix_w_in, attn_sink, ret_decay, mix_w_out, hy_w_in, hy_b_in, hy_short_w, hy_short_b,
              hy_f0, hy_fb0, hy_f1, hy_fb1, hy_f2, hy_fb2, hy_f3, hy_freq, hy_bias, hy_w_out):
    Bn, L, D = x.shape
    rope_a = axial_rope(L)
    rope_r = line_rope(L, R_DIM)
    sc = jax.nn.silu(c)
    scc = jax.nn.silu(c_ctx)[None]
    last_reader = DEPTH - 1 if (DEPTH - 1) % 2 == 0 else DEPTH - 2
    for l in range(DEPTH):
        ctx_live = l <= last_reader
        ctx_full = l < last_reader
        m = (sc @ w_mod[l] + b_mod[l]).reshape(Bn, 1, N_MOD, D)
        mc = (scc @ w_mod[l] + b_mod[l]).reshape(1, 1, N_MOD, D)
        x = macaron_half(x, m, 0, norm_pre[l, 0], norm_post[l, 0], ffn_gate[l, 0], ffn_up[l, 0], ffn_down[l, 0])
        if ctx_live:
            ctx = macaron_half(ctx, mc, 0, norm_pre[l, 0], norm_post[l, 0],
                               ffn_gate[l, 0], ffn_up[l, 0], ffn_down[l, 0])
        h = adaln_in(x, norm_pre[l, 1], m, 1)
        hc = adaln_in(ctx, norm_pre[l, 1], mc, 1) if ctx_live else None
        if l % 2 == 0:
            e = l // 2
            y, yc = even_mixer(h, hc, mix_w_in[e], attn_sink[e], ret_decay[e], mix_w_out[e],
                               rope_a, rope_r, ctx_full)
        else:
            o = l // 2
            hp = (hy_w_in[o], hy_b_in[o], hy_short_w[o], hy_short_b[o], hy_f0[o], hy_fb0[o], hy_f1[o],
                  hy_fb1[o], hy_f2[o], hy_fb2[o], hy_f3[o], hy_freq[o], hy_bias[o], hy_w_out[o])
            y = hyena_mixer(h, *hp)
            yc = hyena_mixer(hc, *hp) if ctx_full else None
        x = adaln_out(x, y, norm_post[l, 1], m, 1, 1.0)
        x = macaron_half(x, m, 2, norm_pre[l, 2], norm_post[l, 2], ffn_gate[l, 1], ffn_up[l, 1], ffn_down[l, 1])
        if ctx_full:
            ctx = adaln_out(ctx, yc, norm_post[l, 1], mc, 1, 1.0)
            ctx = macaron_half(ctx, mc, 2, norm_pre[l, 2], norm_post[l, 2],
                               ffn_gate[l, 1], ffn_up[l, 1], ffn_down[l, 1])
    return x


_drawn_inputs = setup_inputs


def setup_inputs(seed=0):
    import zlib

    import numpy as np

    out = dict(_drawn_inputs(seed))
    spreads = {}
    factors = {'norm_pre': 3.172,
     'norm_post': 5.307,
     'attn_sink': 64.0,
     'hy_b_in': 6.024,
     'hy_short_b': 5.597,
     'hy_fb0': 4.56,
     'hy_fb1': 4.791,
     'hy_fb2': 2.941,
     'hy_freq': 8.0}
    for name, (base, spread) in spreads.items():
        noise = np.random.default_rng([zlib.crc32(name.encode()), seed]).standard_normal(out[name].shape)
        drawn = base * np.exp(spread * noise) if base else spread * noise
        out[name] = jnp.asarray(drawn.astype(out[name].dtype))
    for name, factor in factors.items():
        out[name] = (out[name] * factor).astype(out[name].dtype)
    return out
```

```python
from contextlib import ExitStack
import math

import numpy as np

import concourse.bass as bass
from concourse import mybir

F32 = mybir.dt.float32
F32R = mybir.dt.float32r
ALU = mybir.AluOpType
ACT = mybir.ActivationFunctionType
AX = mybir.AxisListType

P = 128
D = 1024
KT = D // P
SEQ = 512
CTX = 256
ALL = SEQ + CTX
D_FF = 2816
FT = D_FF // P
HALF_TILES = (12, 10)
HEAD = 64
HEADS = 8
EPS = 1e-6
NEG = -1e30
QK_SCALE = HEAD ** -0.5
RING = 4
BANKS = 4
IN_TILES = 22
MASK_W = 3 * P
G_LOW = -2 * P
G_W = 11 * P
HB = 256
POS_TILES = 8
HID = 64
EMB = 33
NMOD = 9
SHIFT, SCALE, GATE = range(3)

AK, AV, AQ, RV, RK, RQ, RG = [12], [13], [0, 1, 2, 3], [18, 19, 20, 21], [14, 15, 16, 17], [4, 5, 6, 7], [8, 9, 10, 11]
ORDER = AK + AV + AQ + RV + RK + RQ + RG
WITH_CTX = AK + AV + RV + RK
ROTATED = [t for t in ORDER if t in AK + AQ + RK + RQ]
VALUES = AV + RV
UNITS = HEADS * (SEQ // P)
KEY_TILES = ALL // P


def stepped(eng, n, body):
    body(0, False)
    if n > 2:
        with eng.Fori(1, n - 1) as i:
            body(i, False)
    body(n - 1, True)


class Stage:

    def __init__(self, src, blocks, cols, mods=None):
        self.src, self.blocks, self.cols, self.mods = src, blocks, cols, mods
        self.first = 0


def build(nc, io):
    stages = []

    def stage(name, src, blocks, cols, mods=None):
        s = Stage(src, blocks, cols, mods)
        s.first = stages[-1][1].first + stages[-1][1].blocks if stages else 0
        stages.append((name, s))
        return s

    ffns = []
    for which, (half0, half1, down1) in [(0, ((0, 2), None, None)), (0, (None, None, None))]:
        ffns.append([stage("gu", io["gate_up"][which, 0:24], 24, 1024, half0),
                     stage("dn", io["down_a"][which], 16, 768),
                     stage("gu", io["gate_up"][which, 24:44], 20, 1024, half1),
                     stage("dn", io["down_b"][which], 16, 640, down1)])
    mix_in = stage("mix_in", io["mix_in"], IN_TILES, 1024)
    mix_out = stage("mix_out", io["mix_out"], KT, 1024)
    for which, (half0, half1, down1) in [(1, (None, (1, 0), (1, 5))), (2, (None, None, None))]:
        ffns.append([stage("gu", io["gate_up"][which, 0:24], 24, 1024, half0),
                     stage("dn", io["down_a"][which], 16, 768),
                     stage("gu", io["gate_up"][which, 24:44], 20, 1024, half1),
                     stage("dn", io["down_b"][which], 16, 640, down1)])
    hy_in = stage("hy_in", io["hy_in"], 24, 1024)
    hy_out = stage("hy_out", io["hy_out"], KT, 1024)
    ffns.append([stage("gu", io["gate_up"][3, 0:24], 24, 1024),
                 stage("dn", io["down_a"][3], 16, 768),
                 stage("gu", io["gate_up"][3, 24:44], 20, 1024),
                 stage("dn", io["down_b"][3], 16, 640)])
    total_blocks = stages[-1][1].first + stages[-1][1].blocks

    def cols_of(b):
        return next(s.cols for _, s in stages if s.first <= b < s.first + s.blocks)

    with ExitStack() as ctx:
        def sb(name, shape, dt=F32):
            return ctx.enter_context(nc.sbuf_tensor(name, shape, dt))

        def sem(name):
            return ctx.enter_context(nc.semaphore(name))

        with ExitStack() as r:
            h_hi = r.enter_context(nc.sbuf_tensor("h_hi", [P, KT, SEQ], F32R))
            h_lo = r.enter_context(nc.sbuf_tensor("h_lo", [P, KT, SEQ], F32R))
        filt = sb("filt", [P, 3, 4, 512])
        term = sb("term", [P, 2, 1024])
        x = sb("x", [P, KT, SEQ])
        raw = sb("raw", [P, RING, 1024])
        w_hi = sb("w_hi", [P, RING, 1024], F32R)
        w_lo = sb("w_lo", [P, RING, 1024], F32R)
        mod = sb("mod", [P, 2, NMOD, 2, KT])
        gain_in = sb("gain_in", [P, 2, 3, 2, KT])
        gain_out = sb("gain_out", [P, 2, 3, 2, KT])
        b_mod = sb("b_mod", [P, 2, NMOD, KT])
        g_pre = sb("g_pre", [P, 2, 3, KT])
        g_post = sb("g_post", [P, 2, 3, KT])
        c_cols = sb("c_cols", [P, KT, 2])
        c_silu = sb("c_silu", [P, KT, 32])
        ident = sb("ident", [P, P])
        ones = sb("ones", [P, P])
        eps = sb("eps", [P, 1])
        prod = sb("prod", [P, 2, SEQ])
        square = sb("square", [P, 2, SEQ])
        sumsq = sb("sumsq", [P, SEQ])
        rms = sb("rms", [P, 4])
        rinv = sb("rinv", [P, 4])
        full = sb("full", [P, 2, SEQ])
        rinv_wide = full[:, 0, :].rearrange("p (t c) -> p t c", t=4)
        rot = sb("rot", [P, P])
        head_ones = sb("head_ones", [P, P])
        sign = sb("sign", [P, 2])
        sink = sb("sink", [P, HEADS])
        ret = sb("ret", [P, 2 * HEADS])
        log_decay = sb("log_decay", [P, 2 * HEADS])
        ls = sb("ls", [P, 6, 2 * HEADS])
        stats = sb("stats", [P, 2, 8])
        filt_dram = nc.dram_tensor("filt_dram", (2, P, 3, 4, 512), F32).ap()

        scopes = []

        class region:

            def __enter__(self):
                scopes.append(ExitStack())

            def __exit__(self, *_):
                scopes.pop().close()

        def rb(name, shape, dt=F32):
            return scopes[-1].enter_context(nc.sbuf_tensor(name, shape, dt))

        with region():
            cx = rb("cx", [P, KT, CTX])
            y = rb("y", [P, KT, SEQ])
            act_hi = rb("act_hi", [P, 12, SEQ], F32R)
            act_lo = rb("act_lo", [P, 12, SEQ], F32R)
            silu = square
            mod_raw = rb("mod_raw", [P, RING, 1024])
            mod_row = rb("mod_row", [P, 256])
        with region():
            rg = rb("rg", [P, 4, SEQ])
            rq = rb("rq", [P, HEADS, SEQ])
            rk = rb("rk", [P, 4, ALL])
            rv = rb("rv", [P, ALL // P, 512])
            av = rb("av", [P, ALL // P, P])
            with region():
                aq = rb("aq", [P, 4, SEQ])
                ak = rb("ak", [P, 4, ALL])
                with region():
                    hc_hi = rb("hc_hi", [P, KT, CTX], F32R)
                    hc_lo = rb("hc_lo", [P, KT, CTX], F32R)
                    rope = rb("rope", [P, 2, SEQ])
                with region():
                    mask = rb("mask", [P, MASK_W])
                    scores = rb("scores", [P, 2, 640])
                    probs = rb("probs", [P, 2, 640])
                    probs_t = rb("probs_t", [P, 2, 640])
            with region():
                dist = rb("dist", [P, G_W])
                arg = rb("arg", [P, G_W])
                decay = rb("decay", [P, 2, G_W])
                decay_ctx = rb("decay_ctx", [P, 2, 2, SEQ])
                att = rb("att", [P, 3, SEQ])
        with region():
            pos = rb("pos", [EMB, 1024])
            hid = rb("hid", [P, 2, 1024])
            hid_t = rb("hid_t", [HID, 1024])
            f0 = rb("f0", [EMB, HID])
            f12 = rb("f12", [HID, 2, HID])
            fb = rb("fb", [HID, 4])
            f3 = rb("f3", [P, 2 * D])
            taps = rb("taps", [P, POS_TILES, 512])
            taper = rb("taper", [P, 2, 512])
            dft_f = rb("dft_f", [P, 2, 4, P])
            piece = rb("piece", [P, 2, 4, 512])
        with region():
            x0 = rb("x0", [P, KT, SEQ])
            u_t = rb("u_t", [P, KT, SEQ])
            u = rb("u", [P, 4, D])
            hy_cols = rb("hy_cols", [P, 5, 24])
            hy_bias = rb("hy_bias", [P, KT])
            with region():
                zp = rb("zp", [P, 2, SEQ + 2])
                short = rb("short", [P, 3, SEQ])
            with region():
                dft = rb("dft", [P, 2, 4, P])
                idft = rb("idft", [P, 4, HB])
                u_f = rb("u_f", [P, 2, 4, 512])
                y_f = rb("y_f", [P, 2, 4, 512])
        psum = ctx.enter_context(nc.psum_tensor("psum", [P, 8, 512], F32))
        DOWN_BANK, STAT, RBC, MODP, MODT = (4, 3), 5, 5, 6, 7

        raw_landed = [sem(f"raw_landed{i}") for i in range(RING)]
        hi_split, lo_split, block_done, result_read = map(sem, ("hi_split", "lo_split", "block_done", "result_read"))
        silu_ready, act_hi_ready, act_ready = map(sem, ("silu_ready", "act_hi_ready", "act_ready"))
        mod_landed = [sem(f"mod_landed{i}") for i in range(RING)]
        mod_used, mod_row_ready, mod_turned, mod_ready = map(
            sem, ("mod_used", "mod_row_ready", "mod_turned", "mod_ready"))
        loaded, zeroed, c_ready = sem("loaded"), sem("zeroed"), sem("c_ready")
        square_ready, square_used = sem("square_ready"), sem("square_used")
        stat_ready, rms_ready, rinv_ready, wide_ready, rbc_ready = map(
            sem, ("stat_ready", "rms_ready", "rinv_ready", "wide_ready", "rbc_ready"))
        norm_ready, full_ready, h_hi_ready, h_ready, x_ready = map(
            sem, ("norm_ready", "full_ready", "h_hi_ready", "h_ready", "x_ready"))
        stored = sem("stored")
        side_loaded, padded, dve_step = sem("side_loaded"), sem("padded"), sem("dve_step")
        z_copied, rot_ready, roped = sem("z_copied"), sem("rot_ready"), sem("roped")
        v_copied, v_turned, v_ready, gate_ready = sem("v_copied"), sem("v_turned"), sem("v_ready"), sem("gate_ready")
        scores_ready, scores_read, exp_ready, probs_ready = map(sem, ("scores_ready", "scores_read", "exp_ready", "probs_ready"))
        probs_turned, probs_t_ready, pv_done = map(sem, ("probs_turned", "probs_t_ready", "pv_done"))
        out_hi_ready, out_ready = sem("out_hi_ready"), sem("out_ready")
        ls_in, ls_exp = sem("ls_in"), sem("ls_exp")
        arg_ready, decay_exp, decay_ready = sem("arg_ready"), sem("decay_exp"), sem("decay_ready")
        ret_scores, att_ready, ret_done = sem("ret_scores"), sem("att_ready"), sem("ret_done")
        hid_sum, hid_arg, hid_ready = sem("hid_sum"), sem("hid_arg"), sem("hid_ready")
        taps_sum, taps_ready, taper_landed = sem("taps_sum"), sem("taps_ready"), [sem("taper_landed0"), sem("taper_landed1")]
        piece_sum, piece_ready, filt_ready, filt_stored = map(sem, ("piece_sum", "piece_ready", "filt_ready", "filt_stored"))
        z_ready, mid_ready, conv_done, u_t_ready = map(sem, ("z_ready", "mid_ready", "conv_done", "u_t_ready"))
        u_turned, u_ready, filt_loaded = sem("u_turned"), sem("u_ready"), sem("filt_loaded")
        uf_sum, uf_ready, yf_ready, yf_pool_ready = map(sem, ("uf_sum", "uf_ready", "yf_ready", "yf_pool_ready"))
        back_ready, g_ready, g_hi_ready, g_split = map(sem, ("back_ready", "g_ready", "g_hi_ready", "g_split"))
        pool_step = sem("pool_step")
        osq_ready, osum_ready, orms_ready, oval_ready = map(sem, ("osq_ready", "osum_ready", "orms_ready", "oval_ready"))

        def products(eng, step_sem, step, i, part, t0, t1, done, before):
            def flat(v):
                return v.rearrange("p m c -> p (m c)")
            pairs = []
            for j in range(2):
                k_re, k_im = flat(filt[:, i - j + 1, 0:2, :]), flat(filt[:, i - j + 1, 2:4, :])
                u_re, u_im = flat(u_f[:, j, 0:2, :]), flat(u_f[:, j, 2:4, :])
                pairs += ([(k_re, u_re, ALU.add), (k_im, u_im, ALU.subtract)] if part == 0 else
                          [(k_re, u_im, ALU.add), (k_im, u_re, ALU.add)])
            out = flat(y_f[:, i, 2 * part:2 * part + 2, :])
            terms = [out, t0, t1, t0]
            made = [0] * 4
            if before:
                eng.wait_ge(done, before)

            def make(n):
                nonlocal step
                eng.tensor_tensor(terms[n], pairs[n][0], pairs[n][1], ALU.mult).then_inc(step_sem, 1)
                step += 1
                made[n] = step

            def add(n, last=False):
                nonlocal step
                eng.wait_ge(step_sem, step if n > 1 else made[n])
                ins = eng.tensor_tensor(out, out, terms[n], pairs[n][2])
                ins.then_inc(done if last else step_sem, 1)
                step += 0 if last else 1

            make(0)
            make(1)
            make(2)
            add(1)
            eng.wait_ge(step_sem, step)
            make(3)
            add(2)
            add(3, last=True)
            return step

        LOADS = 12
        block = ctx.enter_context(nc.Block())

        @block.sync
        def _(sp):
            for dst, src in ((c_cols, "c_cols"), (x, "x"), (ident, "ident"), (b_mod, "b_mod"), (g_pre, "g_pre"),
                             (g_post, "g_post"), (cx, "ctx"), (rot, "rot"), (head_ones, "head_ones"), (sign, "sign"),
                             (sink, "sink"), (ret, "ret")):
                v = dst[:]
                sp.dma_start(v, io[src]).then_inc(loaded, 16)

            state = {"unit": 0}

            def load_block(b, rel, first, src):
                slot = (first + rel) % RING
                sp.wait_ge(lo_split, b + 1)
                sp.dma_start(raw[:, slot, 0:src.shape[-1]], src).then_inc(raw_landed[slot], 16)

            def load_mod(u, src):
                sp.wait_ge(mod_used, u[0] + 1)
                sp.dma_start(mod_raw[:, u[1], :], src).then_inc(mod_landed[u[1]], 16)

            def mod_group(layer, v):
                for k in range(8):
                    load_mod((state["unit"] + k, k % RING), io["w_mod"][layer, v, k])
                state["unit"] += 8

            def run_stage(s, extra=None):
                first = s.first

                def step(i, last):
                    for j in range(4):
                        if j == 2 and isinstance(i, int) and i == 0 and extra:
                            mod_group(*extra)
                        load_block(first + 4 * i + j, j, first, s.src[4 * i + j])
                        if s.mods:
                            layer, v = s.mods
                            for k in ((0, 1, 2), (3, 4, 5), (6, 7), ())[j]:
                                load_mod((state["unit"] + 8 * i + k, k % RING), io["w_mod"][layer, v + i, k])
                if s.blocks % 4 == 0:
                    stepped(sp, s.blocks // 4, step)
                else:
                    for b in range(s.blocks):
                        load_block(first + b, b, first, s.src[b])
                if s.mods:
                    state["unit"] += 8 * (s.blocks // 4)

            mod_group(0, 0)
            mod_group(0, 1)
            for s in ffns[0]:
                run_stage(s)
            for s in ffns[1]:
                run_stage(s, (0, 8) if s is ffns[1][0] else None)
            run_stage(mix_in)
            run_stage(mix_out)
            for ss in ffns[2:4]:
                for s in ss:
                    run_stage(s)
            run_stage(hy_in)
            run_stage(hy_out)
            for s in ffns[4]:
                run_stage(s)
            for d in range(KT):
                sp.wait_ge(x_ready, 48 + d + 1)
                sp.dma_start(io["out"][:, d], x[:, d, :]).then_inc(stored, 16)
            sp.wait_ge(stored, 16 * KT)

        @block.tensor
        def _(pe):
            at = {"b": 0, "p": 0, "f": 0, "unit": 0, "group": 0, "norm": 0, "h": 0}
            pe.sem_inc(block_done, RING)
            pe.sem_inc(mod_used, RING)

            def three(out, w, cols, hi, lo, start, stop):
                slot, c = w
                pe.matmul(out, w_hi[:, slot, c:c + P], hi, start=start, stop=False)
                pe.matmul(out, w_hi[:, slot, c:c + P], lo, start=False, stop=False)
                return pe.matmul(out, w_lo[:, slot, c:c + P], hi, start=False, stop=stop)

            def mod_unit(u, k, uslot_round):
                pe.wait_ge(mod_landed[k % RING], 16 * uslot_round)
                for j in range(4):
                    ins = pe.matmul(psum[32 * j:32 * j + 32, MODP, 0:256], c_silu[:, k, :],
                                    mod_raw[:, k % RING, 256 * j:256 * j + 256],
                                    start=(k == 0), stop=(k == 7), tile_position=(0, 32 * j))
                ins.then_inc(mod_used, 1)
                return ins

            def mod_units(base, g, ks):
                for k in ks:
                    ins = mod_unit(None, k, 2 * g + k // RING + 1)

            def mod_turn(g):
                pe.wait_ge(mod_row_ready, g + 1)
                for half in range(2):
                    ins = pe.transpose(psum[:, MODT, half * P:half * P + P], mod_row[:, half * P:half * P + P], ident[:, :])
                ins.then_inc(mod_turned, 1)

            def mod_group():
                g = at["group"]
                mod_units(8 * g, g, list(range(8)))
                mod_turn(g)
                at["group"] += 1

            def gate_up(s, T, fresh):
                b0, p0, g0 = s.first, at["p"], at["group"]
                h0 = at["h"]

                def step(i, last):
                    for j in range(4):
                        pe.wait_ge(lo_split, RING + b0 + 4 * i + j + 1)
                        pe.wait_ge(result_read, p0 + 4 * i + j + 1)
                        bank = (p0 + j) % 4
                        slot = (b0 + j) % RING
                        for k in range(KT):
                            if j == 0:
                                pe.wait_ge(h_ready, h0 - KT + k + 1)
                            ins = three(psum[:, bank, 0:T], (slot, k * P), P, h_hi[:, k, 0:T], h_lo[:, k, 0:T],
                                        k == 0, k == KT - 1)
                        ins.then_inc(block_done, 1)
                        if s.mods:
                            mod_units(8 * (g0 + i), g0 + i, ((0, 1, 2), (3, 4, 5), (6, 7), ())[j])
                    if s.mods:
                        mod_turn(g0 + i)
                stepped(pe, s.blocks // 4, step)
                at["p"] += s.blocks
                at["f"] += s.blocks // 2
                if s.mods:
                    at["group"] += s.blocks // 4

            def down(s, T, tiles):
                b0, p0, g0, f0 = s.first, at["p"], at["group"], at["f"] - tiles
                per = tiles // 2

                def step(i, last):
                    for dd in range(2):
                        bank = DOWN_BANK[dd]
                        if dd or not isinstance(i, int) or i:
                            pe.wait_ge(result_read, BANKS + p0 + 2 * i + dd - 1)
                        for half in range(2):
                            j = 2 * dd + half
                            slot = (b0 + j) % RING
                            pe.wait_ge(lo_split, RING + b0 + 4 * i + j + 1)
                            for t in range(per):
                                f = half * per + t
                                if dd == 0 and (f == 0 or f == tiles - 1):
                                    pe.wait_ge(act_ready, f0 + (tiles - 1 if f == 0 else tiles))
                                ins = three(psum[:, bank, 0:T], (slot, t * P), P, act_hi[:, f, 0:T], act_lo[:, f, 0:T],
                                            f == 0, f == tiles - 1)
                            ins.then_inc(block_done, 1)
                            if s.mods:
                                mod_units(8 * (g0 + i), g0 + i, ((0, 1, 2), (3, 4, 5), (6, 7), ())[j])
                    if s.mods:
                        mod_turn(g0 + i)
                stepped(pe, s.blocks // 4, step)
                at["p"] += s.blocks // 2
                if s.mods:
                    at["group"] += s.blocks // 4

            def norm(T, fill=False):
                n = at["norm"]
                nt = T // P
                pe.wait_ge(square_used, KT * (n + 1))
                for t in range(nt):
                    ins = pe.matmul(psum[:, STAT, t:t + 1], sumsq[:, t * P:t * P + P], ones[:, 0:1], start=True, stop=True)
                ins.then_inc(stat_ready, 1)
                if fill:
                    mod_units(8 * at["group"], at["group"], list(range(8)))
                pe.wait_ge(wide_ready, n + 1)
                for t in range(nt):
                    ins = pe.matmul(psum[:, RBC, t * P:t * P + P], rinv_wide[:, t, :], ident[:, :], start=True, stop=True)
                ins.then_inc(rbc_ready, 1)
                at["norm"] += 1
                if fill:
                    mod_turn(at["group"])
                    at["group"] += 1

            def ffn(ss, T):
                norm(T)
                at["h"] += KT
                gate_up(ss[0], T, True)
                down(ss[1], T, HALF_TILES[0])
                gate_up(ss[2], T, False)
                down(ss[3], T, HALF_TILES[1])
                norm(T, fill=ss is ffns[0])

            pe.wait_ge(zeroed, 3)
            pe.wait_ge(c_ready, 1)
            pe.wait_ge(loaded, 16 * LOADS)
            mod_group()
            mod_group()
            ffn(ffns[0], SEQ)
            ffn(ffns[1], CTX)

            def mixer_in():
                norm(CTX)
                norm(SEQ)
                at["h"] += 2 * KT
                rotated = values = 0

                def after(tile):
                    nonlocal rotated, values
                    if tile in ROTATED:
                        pe.wait_ge(z_copied, rotated + 1)
                        if rotated >= 2:
                            pe.wait_ge(roped, rotated - 1)
                        pe.matmul(psum[:, 4 + rotated % 2, :], rot[:, :], full[:, rotated % 2, :],
                                  start=True, stop=True).then_inc(rot_ready, 1)
                        rotated += 1
                    if tile in VALUES:
                        pe.wait_ge(v_copied, values + 1)
                        if values:
                            pe.wait_ge(v_ready, values)
                        for t in range(KEY_TILES):
                            src = sumsq[:, t * P:t * P + P] if t < 4 else prod[:, 1, (t - 4) * P:(t - 3) * P]
                            ins = pe.transpose(psum[:, 6 + t // 4, t % 4 * P:t % 4 * P + P], src, ident[:, :])
                        ins.then_inc(v_turned, 1)
                        values += 1

                for n, tile in enumerate(ORDER):
                    b = mix_in.first + n
                    pe.wait_ge(lo_split, RING + b + 1)
                    for T, hi, lo in ((SEQ, h_hi, h_lo), (CTX, hc_hi, hc_lo))[:2 if tile in WITH_CTX else 1]:
                        pe.wait_ge(result_read, at["p"] + 1)
                        for k in range(KT):
                            if n == 0:
                                pe.wait_ge(h_ready, at["h"] - (KT if T == SEQ else 2 * KT) + k + 1)
                            ins = three(psum[:, at["p"] % 4, 0:T], (b % RING, k * P), P, hi[:, k, 0:T], lo[:, k, 0:T],
                                        k == 0, k == KT - 1)
                        at["p"] += 1
                    ins.then_inc(block_done, 1)
                    if n:
                        after(ORDER[n - 1])
                after(ORDER[-1])

            def attention():
                pe.wait_ge(padded, 2)
                pe.wait_ge(roped, 5)
                pe.wait_ge(v_ready, 1)

                def score(u):
                    h, n = divmod(u, 4)
                    lo, hi = max(n - 1, 0), min(n + 2, 4)
                    k = ak[:, 2 * (h // 4) + h % 2, :]
                    q = aq[:, h // 2, n * P:n * P + P]
                    if u >= 2:
                        pe.wait_ge(scores_read, u - 1)
                    else:
                        pe.wait_ge(result_read, at["p"] + BANKS)
                    a = 2 * (u % 2)
                    pe.matmul(psum[:, a, 0:(hi - lo) * P], q, k[:, lo * P:hi * P], start=True, stop=True)
                    pe.matmul(psum[:, a + 1, 0:CTX], q, k[:, SEQ:ALL], start=True, stop=True).then_inc(scores_ready, 1)

                def turn(u):
                    n = u % 4
                    w = (min(n + 2, 4) - max(n - 1, 0)) + 2
                    pe.wait_ge(probs_ready, u + 1)
                    if u:
                        pe.wait_ge(probs_t_ready, u)
                    for t in range(w):
                        ins = pe.transpose(psum[:, 4 + t // 4, t % 4 * P:t % 4 * P + P], probs[:, u % 2, t * P:t * P + P],
                                           ident[:, :])
                    ins.then_inc(probs_turned, 1)

                def pv(u):
                    h, n = divmod(u, 4)
                    lo, hi = max(n - 1, 0), min(n + 2, 4)
                    keys = list(range(lo, hi)) + [4, 5]
                    r0 = HEAD * (h % 2)
                    pe.wait_ge(probs_t_ready, u + 1)
                    if u % 8 == 0 and u >= 16:
                        pe.wait_ge(out_ready, u // 8 - 1)
                    for t, key in enumerate(keys):
                        ins = pe.matmul(psum[r0:r0 + HEAD, 6 + h // 2 % 2, n * P:n * P + P],
                                        av[:, key, HEAD * (h // 4):HEAD * (h // 4) + HEAD], probs_t[:, u % 2, t * P:t * P + P],
                                        start=(t == 0), stop=(t == len(keys) - 1))
                    ins.then_inc(pv_done, 1)

                for step in range(UNITS + 2):
                    if step < UNITS:
                        score(step)
                    if 0 <= step - 1 < UNITS:
                        turn(step - 1)
                    if step >= 2:
                        pv(step - 2)

            def retention():
                pe.wait_ge(roped, len(ROTATED))
                pe.wait_ge(v_ready, len(VALUES))
                total = HEADS * KEY_TILES
                pe.wait_ge(out_ready, 2)
                pe.wait_ge(scores_read, UNITS)

                def score(i):
                    h, j = divmod(i, KEY_TILES)
                    if i >= 4:
                        pe.wait_ge(att_ready, i - 3)
                    pe.matmul(psum[:, i % 4, :], rk[:, h // 2, j * P:j * P + P], rq[:, h, :],
                              start=True, stop=True).then_inc(ret_scores, 1)

                def value(i):
                    h, j = divmod(i, KEY_TILES)
                    r0 = HEAD * (h % 2)
                    pe.wait_ge(att_ready, i + 1)
                    if j == 0 and h % 2 == 0:
                        pe.wait_ge(out_ready, 4 + h // 2 - 1 if h >= 4 else 3 + h // 2)
                    pe.matmul(psum[r0:r0 + HEAD, 6 + h // 2 % 2, :], rv[:, j, h * HEAD:h * HEAD + HEAD], att[:, i % 3, :],
                              start=(j == 0), stop=(j == KEY_TILES - 1)).then_inc(ret_done, 1)

                def sums(t):
                    pe.wait_ge(osq_ready, t + 1)
                    pe.matmul(psum[:, 4 + t % 2, :], head_ones[:, :], square[:, t % 2, :], start=True, stop=True).then_inc(osum_ready, 1)

                for i in range(total + 2):
                    if i < total:
                        score(i)
                    if i >= 2:
                        value(i - 2)
                    if i >= 15 and (i - 15) % 12 == 0:
                        sums((i - 15) // 12)
                sums(3)

            def project(s, ready):
                for d in range(s.blocks):
                    b = s.first + d
                    pe.wait_ge(lo_split, RING + b + 1)
                    pe.wait_ge(result_read, at["p"] + 1)
                    for k in range(KT):
                        if d == 0:
                            ready(k)
                        ins = three(psum[:, at["p"] % 4, :], (b % RING, k * P), P, h_hi[:, k, :], h_lo[:, k, :],
                                    k == 0, k == KT - 1)
                    ins.then_inc(block_done, 1)
                    at["p"] += 1

            mixer_in()
            attention()
            retention()
            project(mix_out, lambda k: pe.wait_ge(out_ready, k + 1))
            norm(SEQ)

            ffn(ffns[2], SEQ)
            ffn(ffns[3], SEQ)

            def make_filter():
                pe.wait_ge(side_loaded, 16 * 11)
                pe.wait_ge(padded, 4)
                pe.wait_ge(result_read, at["p"] + BANKS)
                for layer in range(3):
                    if layer:
                        pe.wait_ge(hid_ready, layer)
                    for c in range(2):
                        lhs = f0[:, :] if layer == 0 else f12[:, layer - 1, :]
                        rhs = pos[:, c * 512:c * 512 + 512] if layer == 0 else hid[0:HID, 0, c * 512:c * 512 + 512]
                        ins = pe.matmul(psum[0:HID, 6 + c, :], lhs, rhs, start=True, stop=True)
                    ins.then_inc(hid_sum, 1)
                pe.wait_ge(hid_ready, 3)
                for c in range(2):
                    for t in range(POS_TILES):
                        n = c * POS_TILES + t
                        if n >= 2:
                            pe.wait_ge(taps_ready, n - 1)
                        col = (D if t < 4 else 0) + c * 512
                        pe.matmul(psum[:, 4 + n % 2, :], hid[:, 0, t * P:t * P + P], f3[:, col:col + 512],
                                  start=True, stop=True).then_inc(taps_sum, 1)
                    for a in range(4):
                        n = 4 * c + a
                        pe.wait_ge(taps_ready, POS_TILES * c + 2 * a + 2)
                        if n:
                            pe.wait_ge(piece_ready, n)
                        for m in range(4):
                            for k in range(2):
                                ins = pe.matmul(psum[:, m, :], dft_f[:, k, m, :], taps[:, 2 * a + k, :], start=(k == 0), stop=(k == 1))
                        ins.then_inc(piece_sum, 1)

            def hyena():
                norm(SEQ)
                at["h"] += KT

                def turn(d):
                    pe.wait_ge(u_t_ready, d + 1)
                    if d >= 2:
                        pe.wait_ge(u_ready, d - 1)
                    for t in range(4):
                        ins = pe.transpose(psum[:, 6 + d % 2, t * P:t * P + P], u_t[:, d, t * P:t * P + P], ident[:, :])
                    ins.then_inc(u_turned, 1)

                for n in range(24):
                    b = hy_in.first + n
                    pe.wait_ge(lo_split, RING + b + 1)
                    pe.wait_ge(result_read, at["p"] + 1)
                    for k in range(KT):
                        if n == 0:
                            pe.wait_ge(h_ready, at["h"] - KT + k + 1)
                        ins = three(psum[:, at["p"] % 4, :], (b % RING, k * P), P, h_hi[:, k, :], h_lo[:, k, :],
                                    k == 0, k == KT - 1)
                    ins.then_inc(block_done, 1)
                    at["p"] += 1
                    if n % 3 == 0 and n:
                        turn(n // 3 - 1)
                turn(7)
                pe.wait_ge(side_loaded, 16 * 17)
                pe.wait_ge(u_ready, KT)
                pe.wait_ge(result_read, at["p"] + BANKS)
                for c in range(2):
                    if c:
                        pe.wait_ge(yf_ready, 3)
                        pe.wait_ge(yf_pool_ready, 1)
                    for j in range(2):
                        for m in range(4):
                            n = 8 * c + 4 * j + m
                            if n >= 4:
                                pe.wait_ge(uf_ready, n - 3)
                            for k in range(2):
                                ins = pe.matmul(psum[:, n % 4, :], dft[:, k, m, :], u[:, 2 * j + k, c * 512:c * 512 + 512],
                                                start=(k == 0), stop=(k == 1))
                            ins.then_inc(uf_sum, 1)
                    pe.wait_ge(yf_ready, 3 * c + 3)
                    pe.wait_ge(yf_pool_ready, c + 1)
                    for t in range(4):
                        n = 4 * c + t
                        if n >= 2:
                            pe.wait_ge(g_ready, n - 1)
                        for i in range(2):
                            for m in range(4):
                                ins = pe.matmul(psum[:, 4 + n % 2, i * HB:i * HB + HB], y_f[:, i, m, t * P:t * P + P], idft[:, m, :],
                                                start=(m == 0), stop=(m == 3))
                        ins.then_inc(back_ready, 1)

            make_filter()
            hyena()
            project(hy_out, lambda k: pe.wait_ge(g_split, k + 1))
            norm(SEQ)
            ffn(ffns[4], SEQ)

        @block.scalar
        def _(act):
            at = {"p": 0, "f": 0, "norm": 0, "y": 0, "xr": 0, "pre": 0}

            def split_hi(b0, i, cols):
                slot = b0 % RING
                act.wait_ge(raw_landed[slot], 16 * (i + b0 // RING + 1))
                act.wait_ge(block_done, b0 + 4 * i + 1)
                act.activation(w_hi[:, slot, 0:cols], raw[:, slot, 0:cols], ACT.Copy).then_inc(hi_split, 1)

            def ahead(s, i, rel, last):
                if last and s.first + 4 * i + rel >= total_blocks:
                    return
                cols = cols_of(s.first + 4 * i + rel) if last else s.cols
                split_hi(s.first + rel, i, cols)

            def gate_up(s, T):
                b0, p0, f0 = s.first, at["p"], at["f"]

                def step(i, last):
                    for j in range(2):
                        ahead(s, i, 2 * j + 2, last)
                        ahead(s, i, 2 * j + 3, last)
                        bank = (p0 + 2 * j) % 4
                        act.wait_ge(block_done, RING + b0 + 4 * i + 2 * j + 1)
                        act.activation(silu[:, j, 0:T], psum[:, bank, 0:T], ACT.Silu).then_inc(silu_ready, 1)
                        act.wait_ge(result_read, BANKS + p0 + 4 * i + 2 * j + 2)
                        act.activation(act_hi[:, bass.ds(2 * i + j, 1), 0:T], prod[:, j:j + 1, 0:T],
                                       ACT.Copy).then_inc(act_hi_ready, 1)
                stepped(act, s.blocks // 4, step)
                at["p"] += s.blocks
                at["f"] += s.blocks // 2

            def down(s, T, final):
                n0, p0 = KT * at["norm"], at["p"]

                def step(i, last):
                    for dd in range(2):
                        ahead(s, i, 2 * dd + 2, last)
                        ahead(s, i, 2 * dd + 3, last)
                        if final:
                            act.wait_ge(result_read, BANKS + p0 + 2 * i + dd + 1)
                            act.wait_ge(square_used, n0 + 2 * i + dd - 1)
                            act.activation(square[:, dd:dd + 1, 0:T], y[:, bass.ds(2 * i + dd, 1), 0:T],
                                           ACT.Square).then_inc(square_ready, 1)
                stepped(act, s.blocks // 4, step)
                at["p"] += s.blocks // 2

            def square_x(src, T, base):
                n0 = KT * at["norm"]
                for d in range(KT):
                    if base is not None:
                        act.wait_ge(x_ready, base + d + 1)
                    if n0 + d >= 2:
                        act.wait_ge(square_used, n0 + d - 1)
                    act.activation(square[:, d % 2, 0:T], src[:, d, 0:T], ACT.Square).then_inc(square_ready, 1)

            def norm(T):
                n = at["norm"]
                act.wait_ge(stat_ready, n + 1)
                act.activation(rms[:, 0:T // P], psum[:, STAT, 0:T // P], ACT.Sqrt, bias=eps[:, 0:1],
                               scale=1.0 / D).then_inc(rms_ready, 1)
                at["norm"] += 1

            def adaln_in(T, layer, i, who, hi):
                c0 = KT * at["pre"]
                for d in range(KT):
                    act.wait_ge(norm_ready, c0 + d + 1)
                    if d >= 2:
                        act.wait_ge(h_ready, c0 + d - 1)
                    act.activation(full[:, d % 2, 0:T], prod[:, d % 2, 0:T], ACT.Identity,
                                   bias=mod[:, layer, 3 * i, who, d:d + 1],
                                   scale=gain_in[:, layer, i, who, d:d + 1]).then_inc(full_ready, 1)
                    act.wait_ge(full_ready, c0 + d + 1)
                    act.activation(hi[:, d, 0:T], full[:, d % 2, 0:T], ACT.Copy).then_inc(h_hi_ready, 1)
                at["pre"] += 1

            def ffn(ss, T, layer, i, who, src, fresh, chain):
                if fresh:
                    square_x(src, T, None)
                norm(T)
                adaln_in(T, layer, i, who, h_hi)
                gate_up(ss[0], T)
                down(ss[1], T, False)
                gate_up(ss[2], T)
                down(ss[3], T, True)
                norm(T)
                if chain:
                    square_x(src, T, at["xr"])
                at["xr"] += KT

            act.wait_ge(loaded, 16 * LOADS)
            act.wait_ge(zeroed, 3)
            act.activation(c_silu[:, :, 0:2], c_cols[:], ACT.Silu).then_inc(c_ready, 1)
            for b in range(2):
                split_hi(b, 0, 1024)
            ffn(ffns[0], SEQ, 0, 0, 0, x, True, False)
            ffn(ffns[1], CTX, 0, 0, 1, cx, True, True)

            def split_ahead(b):
                if b + 2 < total_blocks:
                    split_hi(b + 2, 0, cols_of(b + 2))

            def mixer_in():
                norm(CTX)
                adaln_in(CTX, 0, 1, 1, hc_hi)
                square_x(x, SEQ, None)
                norm(SEQ)
                adaln_in(SEQ, 0, 1, 0, h_hi)
                rotated = values = 0
                p = at["p"]

                def turned():
                    nonlocal values
                    act.wait_ge(v_turned, values + 1)
                    dst = av if values == 0 else rv[:, :, (values - 1) * P:values * P]
                    act.activation(dst[:, 0:4, :], psum[:, 6, :].rearrange("p (t c) -> p t c", t=4), ACT.Copy)
                    act.activation(dst[:, 4:6, :], psum[:, 7, 0:CTX].rearrange("p (t c) -> p t c", t=2),
                                   ACT.Copy).then_inc(v_ready, 1)
                    values += 1

                for n, tile in enumerate(ORDER):
                    b = mix_in.first + n
                    split_ahead(b)
                    if n and ORDER[n - 1] in VALUES:
                        turned()
                    if tile in ROTATED:
                        act.wait_ge(block_done, RING + b + 1)
                        if rotated >= 2:
                            act.wait_ge(rot_ready, rotated - 1)
                        act.activation(full[:, rotated % 2, :], psum[:, p % 4, :], ACT.Copy).then_inc(z_copied, 1)
                        rotated += 1
                    p += 2 if tile in WITH_CTX else 1
                at["p"] = p
                act.wait_ge(gate_ready, 1)
                act.activation(rg[:], rg[:], ACT.Silu).then_inc(gate_ready, 1)

            def attention():
                def exps(u):
                    w = (min(u % 4 + 2, 4) - max(u % 4 - 1, 0) + 2) * P
                    i = u % 2
                    act.wait_ge(scores_read, u + 1)
                    act.activation(probs[:, i, 0:w], scores[:, i, 0:w], ACT.Exp, bias=stats[:, i, 1:2],
                                   accum_out=stats[:, i, 2:3])
                    act.activation(stats[:, i, 3:4], sink[:, u // 4:u // 4 + 1], ACT.Exp,
                                   bias=stats[:, i, 1:2]).then_inc(exp_ready, 1)

                def copy_out(u):
                    w = (min(u % 4 + 2, 4) - max(u % 4 - 1, 0) + 2) * P
                    act.wait_ge(probs_turned, u + 1)
                    if u >= 2:
                        act.wait_ge(pv_done, u - 1)
                    flat = psum[:, 4:6, :].rearrange("p b c -> p (b c)")
                    act.activation(probs_t[:, u % 2, 0:w], flat[:, 0:w], ACT.Copy).then_inc(probs_t_ready, 1)

                def out(t):
                    act.wait_ge(pv_done, 8 * t + 8)
                    act.activation(h_hi[:, t, :], psum[:, 6 + t % 2, :], ACT.Copy).then_inc(out_hi_ready, 1)

                for step in range(UNITS + 2):
                    if step < UNITS:
                        exps(step)
                    if 0 <= step - 1 < UNITS:
                        copy_out(step - 1)
                    if step >= 10 and (step - 10) % 8 == 0:
                        out((step - 10) // 8)
                out(3)

            def retention():
                act.wait_ge(ls_in, 1)
                act.activation(ls[:, 1, :], ls[:, 0, :], ACT.Exp, scale=-1.0).then_inc(ls_exp, 1)

                def finish(t):
                    act.wait_ge(ret_done, 2 * KEY_TILES * (t + 1))
                    act.activation(square[:, t % 2, :], psum[:, 6 + t % 2, :], ACT.Square).then_inc(osq_ready, 1)
                    act.wait_ge(osum_ready, t + 1)
                    act.activation(prod[:, t % 2, :], psum[:, 4 + t % 2, :], ACT.Sqrt, bias=eps[:, 0:1],
                                   scale=1.0 / HEAD).then_inc(orms_ready, 1)
                    act.wait_ge(oval_ready, t + 1)
                    act.activation(h_hi[:, 4 + t, :], full[:, t % 2, :], ACT.Copy).then_inc(out_hi_ready, 1)

                def exps(h):
                    act.wait_ge(arg_ready, h + 1)
                    act.activation(decay[:, h % 2, :], arg[:, :], ACT.Exp).then_inc(decay_exp, 1)

                exps(0)
                for h in range(HEADS):
                    if h + 1 < HEADS:
                        exps(h + 1)
                    if h >= 2 and h % 2 == 0:
                        finish(h // 2 - 1)
                finish(3)

            def project(s):
                n0, p0 = KT * at["norm"], at["p"]
                for d in range(KT):
                    split_ahead(s.first + d)
                    act.wait_ge(result_read, BANKS + p0 + d + 1)
                    act.wait_ge(square_used, n0 + d - 1)
                    act.activation(square[:, d % 2, :], y[:, d, :], ACT.Square).then_inc(square_ready, 1)
                at["p"] += KT

            mixer_in()
            attention()
            retention()
            project(mix_out)
            norm(SEQ)
            square_x(x, SEQ, at["xr"])
            at["xr"] += KT

            ffn(ffns[2], SEQ, 0, 2, 0, x, False, True)
            ffn(ffns[3], SEQ, 1, 0, 0, x, False, True)

            def make_filter():
                for layer in range(3):
                    act.wait_ge(hid_arg, layer + 1)
                    act.activation(hid[0:HID, 0, :], hid_t[:, :], ACT.Sin).then_inc(hid_ready, 1)
                for n in range(8):
                    act.wait_ge(piece_sum, n + 1)
                    if n >= 2:
                        act.wait_ge(filt_ready, 3 * ((n - 1) // 4) + (n - 1) % 4)
                    act.activation(piece[:, n % 2], psum[:, 0:4, :], ACT.Copy).then_inc(piece_ready, 1)

            def hyena():
                norm(SEQ)
                adaln_in(SEQ, 1, 1, 0, h_hi)
                act.wait_ge(side_loaded, 16 * 15)
                act.wait_ge(padded, 5)

                def turned(d):
                    act.wait_ge(u_turned, d + 1)
                    act.activation(u[:, :, d * P:d * P + P], psum[:, 6 + d % 2, :].rearrange("p (t c) -> p t c", t=4),
                                   ACT.Copy).then_inc(u_ready, 1)

                for n in range(24):
                    b = hy_in.first + n
                    split_ahead(b)
                    d, kind = divmod(n, 3)
                    col = (8, 16, 0)[kind] + d
                    act.wait_ge(block_done, RING + b + 1)
                    if n >= 2:
                        act.wait_ge(conv_done, n - 1)
                    act.activation(zp[:, n % 2, 1:SEQ + 1], psum[:, at["p"] % 4, :], ACT.Identity,
                                   bias=hy_cols[:, 0, col:col + 1]).then_inc(z_ready, 1)
                    at["p"] += 1
                    act.wait_ge(z_ready, n + 1)
                    if kind == 0 and d:
                        act.wait_ge(u_t_ready, d)
                    dst = x0[:, d, :] if kind == 2 else short[:, kind, :]
                    act.activation(dst, zp[:, n % 2, 1:SEQ + 1], ACT.Identity, bias=hy_cols[:, 4, col:col + 1],
                                   scale=hy_cols[:, 2, col:col + 1]).then_inc(mid_ready, 1)
                    if n % 3 == 1 and n > 3:
                        turned(n // 3 - 1)
                turned(7)
                for c in range(2):
                    if c:
                        act.wait_ge(yf_ready, 3)
                        act.wait_ge(yf_pool_ready, 1)
                    for k in range(8):
                        act.wait_ge(uf_sum, 8 * c + k + 1)
                        act.activation(u_f[:, k // 4, k % 4, :], psum[:, k % 4, :], ACT.Copy).then_inc(uf_ready, 1)
                for d in range(KT):
                    act.wait_ge(g_ready, d + 1)
                    if d == 0:
                        act.wait_ge(yf_ready, 6)
                        act.wait_ge(yf_pool_ready, 2)
                    act.activation(h_hi[:, d, :], u_t[:, d, :], ACT.Copy).then_inc(g_hi_ready, 1)

            make_filter()
            hyena()
            project(hy_out)
            norm(SEQ)
            square_x(x, SEQ, at["xr"])
            at["xr"] += KT
            ffn(ffns[4], SEQ, 1, 2, 0, x, False, False)

        @block.vector
        def _(dve):
            at = {"p": 0, "f": 0, "norm": 0, "y": 0, "xr": 0, "pre": 0, "group": 0, "nr": 0}
            dve.memset(ones[:, :], 1.0).then_inc(zeroed, 1)
            dve.memset(eps[:, :], EPS).then_inc(zeroed, 1)
            dve.memset(c_silu[:], 0.0).then_inc(zeroed, 1)
            dve.sem_inc(lo_split, RING)
            dve.sem_inc(result_read, BANKS)

            def split_lo(b0, i, cols):
                slot = b0 % RING
                dve.wait_ge(hi_split, b0 + 4 * i + 1)
                ins = dve.tensor_tensor(w_lo[:, slot, 0:cols], raw[:, slot, 0:cols], w_hi[:, slot, 0:cols].bitcast(F32),
                                        ALU.subtract)
                ins.then_inc(lo_split, 1)

            def ahead(s, i, rel, last):
                if last and s.first + 4 * i + rel >= total_blocks:
                    return
                cols = cols_of(s.first + 4 * i + rel) if last else s.cols
                split_lo(s.first + rel, i, cols)

            def mod_copy(g):
                dve.wait_ge(mod_used, RING + 8 * g + 8)
                dve.tensor_copy(mod_row[:, :], psum[:, MODP, 0:256]).then_inc(mod_row_ready, 1)

            def mod_finish(g, layer, v):
                dve.wait_ge(mod_turned, g + 1)
                turned = psum[:, MODT, 0:256].rearrange("p (h j c) -> p c j h", h=2, j=4)
                for who in range(2):
                    dst = mod[:, layer, bass.ds(v, 1), who, :].rearrange("p o (j h) -> p (o j) h", h=2)
                    bias = b_mod[:, layer, bass.ds(v, 1), :].rearrange("p o (j h) -> p (o j) h", h=2)
                    ins = dve.tensor_tensor(dst, turned[:, who], bias, ALU.add)
                ins.then_inc(mod_ready, 1)

            def mod_group(layer, v):
                mod_copy(at["group"])
                mod_finish(at["group"], layer, v)
                at["group"] += 1

            def gain_pre(layer, i):
                dve.wait_ge(mod_ready, at["group"])
                for who in range(2):
                    ins = dve.scalar_tensor_tensor(gain_in[:, layer, i, who, :], mod[:, layer, 3 * i + SCALE, who, :], 1.0,
                                                   g_pre[:, layer, i, :], ALU.add, ALU.mult)
                ins.then_inc(dve_step, 1)

            def gain_post(layer, i, w):
                dve.wait_ge(mod_ready, at["group"])
                for who in range(2):
                    ins = dve.scalar_tensor_tensor(gain_out[:, layer, i, who, :], mod[:, layer, 3 * i + GATE, who, :], w,
                                                   g_post[:, layer, i, :], ALU.mult, ALU.mult)
                ins.then_inc(dve_step, 1)

            def gate_up(s, T):
                b0, p0, f0, g0 = s.first, at["p"], at["f"], at["group"]

                def step(i, last):
                    for j in range(2):
                        ahead(s, i, 2 * j + 2, last)
                        ahead(s, i, 2 * j + 3, last)
                        if s.mods and j == 1:
                            mod_copy(g0 + i)
                        bank = (p0 + 2 * j + 1) % 4
                        dve.wait_ge(block_done, RING + b0 + 4 * i + 2 * j + 2)
                        dve.wait_ge(silu_ready, f0 + 2 * i + j + 1)
                        ins = dve.tensor_tensor(prod[:, j, 0:T], psum[:, bank, 0:T], silu[:, j, 0:T], ALU.mult)
                        ins.then_inc(result_read, 2)
                        dve.wait_ge(act_hi_ready, f0 + 2 * i + j + 1)
                        dve.wait_ge(result_read, BANKS + p0 + 4 * i + 2 * j + 2)
                        fl = bass.ds(2 * i + j, 1)
                        dve.tensor_tensor(act_lo[:, fl, 0:T], prod[:, j:j + 1, 0:T], act_hi[:, fl, 0:T].bitcast(F32),
                                          ALU.subtract).then_inc(act_ready, 1)
                    if s.mods:
                        mod_finish(g0 + i, s.mods[0], s.mods[1] + i)
                stepped(dve, s.blocks // 4, step)
                at["p"] += s.blocks
                at["f"] += s.blocks // 2
                if s.mods:
                    at["group"] += s.blocks // 4

            def add_square(n, T, d):
                dve.wait_ge(square_ready, n + 1)
                if d is not None and d == 0:
                    dve.tensor_copy(sumsq[:, 0:T], square[:, 0, 0:T]).then_inc(square_used, 1)
                    return
                dve.wait_ge(square_used, n)
                dve.tensor_tensor(sumsq[:, 0:T], sumsq[:, 0:T], square[:, d % 2, 0:T], ALU.add).then_inc(square_used, 1)

            def down(s, T, final):
                b0, p0, g0, n0 = s.first, at["p"], at["group"], KT * at["norm"]
                if final:
                    dve.memset(sumsq[:, 0:T], 0.0).then_inc(zeroed, 1)
                    at["z"] = at.get("z", 3) + 1
                    dve.wait_ge(zeroed, at["z"])

                def step(i, last):
                    for dd in range(2):
                        ahead(s, i, 2 * dd + 2, last)
                        ahead(s, i, 2 * dd + 3, last)
                        if s.mods and dd == 1:
                            mod_copy(g0 + i)
                        bank = DOWN_BANK[dd]
                        dve.wait_ge(block_done, RING + b0 + 4 * i + 2 * dd + 2)
                        dst = y[:, bass.ds(2 * i + dd, 1), 0:T]
                        src = psum[:, bank:bank + 1, 0:T]
                        if not final:
                            dve.tensor_copy(dst, src).then_inc(result_read, 1)
                        else:
                            ins = dve.tensor_tensor(dst, src, dst, ALU.add)
                            ins.then_inc(result_read, 1)
                            n = n0 + 2 * i + dd
                            dve.wait_ge(square_ready, n + 1)
                            dve.wait_ge(square_used, n)
                            dve.tensor_tensor(sumsq[:, 0:T], sumsq[:, 0:T], square[:, dd, 0:T],
                                              ALU.add).then_inc(square_used, 1)
                    if s.mods:
                        mod_finish(g0 + i, s.mods[0], s.mods[1] + i)
                stepped(dve, s.blocks // 4, step)
                at["p"] += s.blocks // 2
                if s.mods:
                    at["group"] += s.blocks // 4

            def norm(T):
                n = at["norm"]
                nt = T // P
                dve.wait_ge(rms_ready, n + 1)
                dve.reciprocal(rinv[:, 0:nt], rms[:, 0:nt]).then_inc(rinv_ready, 1)
                dve.wait_ge(rinv_ready, n + 1)
                for t in range(nt):
                    ins = dve.tensor_scalar(rinv_wide[:, t, :], ones[:, :], rinv[:, t:t + 1], None, ALU.mult)
                ins.then_inc(wide_ready, 1)
                dve.wait_ge(rbc_ready, n + 1)
                at["norm"] += 1

            def adaln_in(src, T, hi, lo):
                c0 = KT * at["pre"]
                for d in range(KT + 1):
                    if d < KT:
                        dve.tensor_tensor(prod[:, d % 2, 0:T], src[:, d, 0:T], psum[:, RBC, 0:T],
                                          ALU.mult).then_inc(norm_ready, 1)
                    if d >= 1:
                        e = d - 1
                        dve.wait_ge(h_hi_ready, c0 + e + 1)
                        dve.tensor_tensor(lo[:, e, 0:T], full[:, e % 2, 0:T], hi[:, e, 0:T].bitcast(F32),
                                          ALU.subtract).then_inc(h_ready, 1)
                at["pre"] += 1

            def adaln_out(dst, T, layer, i, who, chain):
                n0 = KT * at["norm"]
                r0 = at["nr"]
                for d in range(KT + 1):
                    if d < KT:
                        dve.tensor_tensor(full[:, d % 2, 0:T], y[:, d, 0:T], psum[:, RBC, 0:T],
                                          ALU.mult).then_inc(dve_step, 1)
                        at["step"] += 1
                        dve.wait_ge(dve_step, at["step"])
                        dve.scalar_tensor_tensor(dst[:, d, 0:T], full[:, d % 2, 0:T],
                                                 gain_out[:, layer, i, who, d:d + 1], dst[:, d, 0:T],
                                                 ALU.mult, ALU.add).then_inc(x_ready, 1)
                    if d >= 1 and chain:
                        add_square(n0 + d - 1, T, d - 1)
                at["xr"] += KT

            def ffn(ss, T, layer, i, who, src, fresh, chain):
                if fresh:
                    for d in range(KT):
                        add_square(KT * at["norm"] + d, T, d)
                gain_pre(layer, i)
                at["step"] += 1
                dve.wait_ge(dve_step, at["step"])
                norm(T)
                adaln_in(src, T, h_hi, h_lo)
                gate_up(ss[0], T)
                down(ss[1], T, False)
                gate_up(ss[2], T)
                down(ss[3], T, True)
                norm(T)
                if ss is ffns[0]:
                    mod_copy(at["group"])
                gain_post(layer, i, 0.5)
                at["step"] += 1
                dve.wait_ge(dve_step, at["step"])
                adaln_out(src, T, layer, i, who, chain)
                if ss is ffns[0]:
                    mod_finish(at["group"], 0, 8)
                    at["group"] += 1

            at["step"] = 0
            dve.wait_ge(loaded, 16 * LOADS)
            mod_group(0, 0)
            mod_group(0, 1)
            for b in range(2):
                split_lo(b, 0, 1024)
            ffn(ffns[0], SEQ, 0, 0, 0, x, True, False)

            ffn(ffns[1], CTX, 0, 0, 1, cx, True, True)

            def seq(ins):
                ins.then_inc(dve_step, 1)
                at["step"] += 1
                dve.wait_ge(dve_step, at["step"])

            def split_ahead(b):
                if b + 2 < total_blocks:
                    split_lo(b + 2, 0, cols_of(b + 2))

            def mixer_in():
                gain_pre(0, 1)
                at["step"] += 1
                dve.wait_ge(dve_step, at["step"])
                norm(CTX)
                adaln_in(cx, CTX, hc_hi, hc_lo)
                for d in range(KT):
                    add_square(KT * at["norm"] + d, SEQ, d)
                norm(SEQ)
                adaln_in(x, SEQ, h_hi, h_lo)
                rotated = values = 0
                dve.wait_ge(padded, 2)
                dve.wait_ge(side_loaded, 16)

                def rotate(bank, tile):
                    nonlocal rotated
                    r = rotated % 2
                    if tile == RK[0]:
                        dve.wait_ge(side_loaded, 32)
                    dve.wait_ge(rot_ready, rotated + 1)
                    dve.tensor_tensor(prod[:, r, :], psum[:, bank, :], rope[:, 0, :], ALU.mult).then_inc(result_read, 1)
                    seq(dve.tensor_tensor(square[:, r, :], psum[:, 4 + r, :], rope[:, 1, :], ALU.mult))
                    at["p"] += 1
                    dve.wait_ge(result_read, BANKS + at["p"])
                    if tile in AQ or tile in RK:
                        dst = aq[:, tile, :] if tile in AQ else rk[:, tile - RK[0], 0:SEQ]
                        ins = dve.tensor_tensor(dst, prod[:, r, :], square[:, r, :], ALU.add)
                    elif tile in RQ:
                        for half in range(2):
                            rows = slice(HEAD * half, HEAD * half + HEAD)
                            ins = dve.tensor_tensor(rq[rows, 2 * (tile - RQ[0]) + half, :], prod[rows, r, :], square[rows, r, :], ALU.add)
                    else:
                        for g in range(2):
                            for half in range(2):
                                src, dst = slice(HEAD * g, HEAD * g + HEAD), slice(HEAD * half, HEAD * half + HEAD)
                                ins = dve.tensor_tensor(ak[dst, 2 * g + half, 0:SEQ], prod[src, r, :], square[src, r, :], ALU.add)
                    ins.then_inc(roped, 1)
                    rotated += 1

                for n, tile in enumerate(ORDER):
                    b = mix_in.first + n
                    split_ahead(b)
                    dve.wait_ge(block_done, RING + b + 1)
                    bank = at["p"] % 4
                    if tile in VALUES:
                        if values:
                            dve.wait_ge(v_turned, values)
                        dve.tensor_copy(sumsq[:, :], psum[:, bank, :]).then_inc(result_read, 1)
                        dve.tensor_copy(prod[:, 1, 0:CTX], psum[:, (bank + 1) % 4, 0:CTX]).then_inc(result_read, 1)
                        at["p"] += 2
                        dve.wait_ge(result_read, BANKS + at["p"])
                        dve.sem_inc(v_copied, 1)
                        values += 1
                    elif tile in RG:
                        ins = dve.tensor_copy(rg[:, tile - RG[0], :], psum[:, bank, :])
                        ins.then_inc(result_read, 1)
                        at["p"] += 1
                    elif tile in WITH_CTX:
                        ctx_bank = (bank + 1) % 4
                        if tile in RK:
                            seq(dve.tensor_copy(rk[:, tile - RK[0], SEQ:ALL], psum[:, ctx_bank, 0:CTX]))
                        else:
                            for g in range(2):
                                for half in range(2):
                                    src, dst = slice(HEAD * g, HEAD * g + HEAD), slice(HEAD * half, HEAD * half + HEAD)
                                    ins = dve.tensor_copy(ak[dst, 2 * g + half, SEQ:ALL], psum[src, ctx_bank, 0:CTX])
                            seq(ins)
                        rotate(bank, tile)
                        dve.sem_inc(result_read, 1)
                        at["p"] += 1
                    else:
                        rotate(bank, tile)
                dve.wait_ge(result_read, BANKS + at["p"])
                dve.sem_inc(gate_ready, 1)

            def attention():
                dve.wait_ge(side_loaded, 48)

                def take(u):
                    h, n = divmod(u, 4)
                    lo, hi = max(n - 1, 0), min(n + 2, 4)
                    w = (hi - lo) * P
                    m = (lo - n + 1) * P
                    i = u % 2
                    dve.wait_ge(scores_ready, u + 1)
                    dve.scalar_tensor_tensor(scores[:, i, 0:w], psum[:, 2 * i, 0:w], QK_SCALE, mask[:, m:m + w], ALU.mult, ALU.add)
                    seq(dve.tensor_scalar(scores[:, i, w:w + CTX], psum[:, 2 * i + 1, 0:CTX], QK_SCALE, None, ALU.mult))
                    seq(dve.tensor_reduce(stats[:, i, 0:1], scores[:, i, 0:w + CTX], AX.X, ALU.max))
                    dve.tensor_scalar(stats[:, i, 1:2], stats[:, i, 0:1], sink[:, h:h + 1], -1.0, ALU.max,
                                      ALU.mult).then_inc(scores_read, 1)

                def normalize(u):
                    w = (min(u % 4 + 2, 4) - max(u % 4 - 1, 0) + 2) * P
                    i = u % 2
                    dve.wait_ge(exp_ready, u + 1)
                    seq(dve.tensor_tensor(stats[:, i, 4:5], stats[:, i, 2:3], stats[:, i, 3:4], ALU.add))
                    seq(dve.reciprocal(stats[:, i, 5:6], stats[:, i, 4:5]))
                    dve.tensor_scalar(probs[:, i, 0:w], probs[:, i, 0:w], stats[:, i, 5:6], None, ALU.mult).then_inc(probs_ready, 1)

                def out(t):
                    dve.wait_ge(out_hi_ready, t + 1)
                    dve.tensor_tensor(h_lo[:, t, :], psum[:, 6 + t % 2, :], h_hi[:, t, :].bitcast(F32),
                                      ALU.subtract).then_inc(out_ready, 1)

                for step in range(UNITS + 2):
                    if step < UNITS:
                        take(step)
                    if 0 <= step - 1 < UNITS:
                        normalize(step - 1)
                    if step >= 11 and (step - 11) % 8 == 0:
                        out((step - 11) // 8)
                out(3)

            def log_sigmoid():
                n = 2 * HEADS
                seq(dve.tensor_scalar(ls[:, 2, :], ret[:, :], -1.0, None, ALU.mult))
                dve.tensor_tensor(ls[:, 0, :], ret[:, :], ls[:, 2, :], ALU.max).then_inc(ls_in, 1)
                dve.wait_ge(ls_exp, 1)
                seq(dve.tensor_scalar(ls[:, 2, :], ls[:, 1, :], 2.0, None, ALU.add))
                seq(dve.reciprocal(ls[:, 3, :], ls[:, 2, :]))
                seq(dve.tensor_tensor(ls[:, 4, :], ls[:, 1, :], ls[:, 3, :], ALU.mult))
                seq(dve.tensor_tensor(ls[:, 5, :], ls[:, 4, :], ls[:, 4, :], ALU.mult))
                seq(dve.tensor_scalar(ls[:, 2, :], ls[:, 5, :], 1.0 / 19, None, ALU.mult))
                for k in range(8, 0, -1):
                    seq(dve.scalar_tensor_tensor(ls[:, 2, :], ls[:, 2, :], 1.0 / (2 * k + 1), ls[:, 5, :], ALU.add, ALU.mult))
                seq(dve.scalar_tensor_tensor(ls[:, 3, :], ls[:, 2, :], 1.0, ls[:, 4, :], ALU.add, ALU.mult))
                seq(dve.tensor_scalar(ls[:, 0, :], ret[:, :], 0.0, None, ALU.min))
                seq(dve.scalar_tensor_tensor(log_decay[:, :], ls[:, 3, :], -2.0, ls[:, 0, :], ALU.mult, ALU.add))
                seq(dve.tensor_scalar(log_decay[:, HEADS:n], log_decay[:, HEADS:n], -1.0, None, ALU.mult))

            def retention():
                log_sigmoid()
                dve.wait_ge(side_loaded, 64)

                def table(h):
                    i = h % 2
                    if h:
                        dve.wait_ge(decay_exp, h)
                    dve.tensor_scalar(arg[:, :], dist[:, :], 0.0, log_decay[:, h:h + 1], ALU.max, ALU.mult)
                    seq(dve.tensor_scalar(decay[:, i, :], dist[:, :], 0.0, log_decay[:, HEADS + h:HEADS + h + 1], ALU.min, ALU.mult))
                    dve.tensor_tensor(arg[:, :], arg[:, :], decay[:, i, :], ALU.add).then_inc(arg_ready, 1)
                    dve.wait_ge(decay_exp, h + 1)
                    zero = 3 * P - G_LOW
                    seq(dve.tensor_tensor(decay[:, i, zero:zero + P], decay[:, i, zero:zero + P], ident[:, :], ALU.add))
                    for c in range(2):
                        fwd, bwd = zero + CTX - c * P, zero - SEQ - c * P
                        ins = dve.tensor_tensor(decay_ctx[:, i, c, :], decay[:, i, fwd:fwd + SEQ], decay[:, i, bwd:bwd + SEQ], ALU.add)
                    seq(ins)

                def weigh(i):
                    h, j = divmod(i, KEY_TILES)
                    dve.wait_ge(ret_scores, i + 1)
                    if i >= 3:
                        dve.wait_ge(ret_done, i - 2)
                    zero = 3 * P - G_LOW
                    w = decay[:, h % 2, zero - j * P:zero - j * P + SEQ] if j < 4 else decay_ctx[:, h % 2, j - 4, :]
                    dve.scalar_tensor_tensor(att[:, i % 3, :], psum[:, i % 4, :], QK_SCALE, w, ALU.mult, ALU.mult).then_inc(att_ready, 1)

                def finish(t):
                    dve.wait_ge(orms_ready, t + 1)
                    seq(dve.reciprocal(sumsq[:, :], prod[:, t % 2, :]))
                    seq(dve.tensor_tensor(sumsq[:, :], psum[:, 6 + t % 2, :], sumsq[:, :], ALU.mult))
                    dve.tensor_tensor(full[:, t % 2, :], sumsq[:, :], rg[:, t, :], ALU.mult).then_inc(oval_ready, 1)
                    dve.wait_ge(out_hi_ready, 4 + t + 1)
                    dve.tensor_tensor(h_lo[:, 4 + t, :], full[:, t % 2, :], h_hi[:, 4 + t, :].bitcast(F32),
                                      ALU.subtract).then_inc(out_ready, 1)

                dve.wait_ge(gate_ready, 2)
                table(0)
                for i in range(HEADS * KEY_TILES):
                    h, j = divmod(i, KEY_TILES)
                    weigh(i)
                    if j == 1 and h + 1 < HEADS:
                        table(h + 1)
                    if j == 4 and h >= 2 and h % 2 == 0:
                        finish(h // 2 - 1)
                finish(3)

            def project(s):
                n0, b0 = KT * at["norm"], s.first
                seq(dve.memset(sumsq[:, :], 0.0))
                for d in range(KT):
                    split_ahead(b0 + d)
                    dve.wait_ge(block_done, RING + b0 + d + 1)
                    dve.tensor_copy(y[:, d, :], psum[:, at["p"] % 4, :]).then_inc(result_read, 1)
                    at["p"] += 1
                    dve.wait_ge(square_ready, n0 + d + 1)
                    dve.wait_ge(square_used, n0 + d)
                    dve.tensor_tensor(sumsq[:, :], sumsq[:, :], square[:, d % 2, :], ALU.add).then_inc(square_used, 1)

            def mixer_post(layer):
                norm(SEQ)
                gain_post(layer, 1, 1.0)
                at["step"] += 1
                dve.wait_ge(dve_step, at["step"])
                adaln_out(x, SEQ, layer, 1, 0, True)

            mixer_in()
            attention()
            retention()
            project(mix_out)
            mixer_post(0)

            ffn(ffns[2], SEQ, 0, 2, 0, x, False, True)
            ffn(ffns[3], SEQ, 1, 0, 0, x, False, True)

            def make_filter():
                two_pi = 2.0 * math.pi
                c1 = 6.28125
                c2 = float((np.float32(two_pi - c1).view(np.uint32) & np.uint32(0xFFFFF000)).view(np.float32))
                c3 = two_pi - c1 - c2
                magic = 1.5 * 2 ** 23
                edge = float(np.nextafter(np.float32(math.pi), np.float32(0)))
                a, k = hid_t, hid[0:HID, 1, :]
                for layer in range(3):
                    dve.wait_ge(hid_sum, layer + 1)
                    seq(dve.tensor_scalar(a[:, :], psum[0:HID, 6:8, :].rearrange("p b c -> p (b c)"), fb[:, layer:layer + 1], fb[:, 3:4],
                                          ALU.add, ALU.mult))
                    seq(dve.tensor_scalar(k, a[:, :], 1.0 / two_pi, magic, ALU.mult, ALU.add))
                    seq(dve.tensor_scalar(k, k, magic, None, ALU.subtract))
                    for c in (c1, c2, c3):
                        seq(dve.scalar_tensor_tensor(a[:, :], k, -c, a[:, :], ALU.mult, ALU.add))
                    dve.tensor_scalar(a[:, :], a[:, :], -edge, edge, ALU.max, ALU.min).then_inc(hid_arg, 1)
                for c in range(2):
                    for t in range(POS_TILES):
                        n = c * POS_TILES + t
                        dve.wait_ge(taps_sum, n + 1)
                        dve.wait_ge(taper_landed[n % 2], 16 * (n // 2 + 1))
                        if c:
                            dve.wait_ge(piece_sum, t // 2 + 1)
                        dve.tensor_tensor(taps[:, t, :], psum[:, 4 + n % 2, :], taper[:, n % 2, :], ALU.mult).then_inc(taps_ready, 1)
                    for d in range(3):
                        n = 4 * c + d + 1
                        dve.wait_ge(piece_ready, n + 1)
                        if c and d == 0:
                            dve.wait_ge(filt_stored, 16)
                        new, old = piece[:, n % 2], piece[:, (n - 1) % 2]
                        dve.scalar_tensor_tensor(filt[:, d, 0:2, :], old[:, 2:4, :], sign[:, 1:2], new[:, 0:2, :], ALU.mult, ALU.add)
                        dve.scalar_tensor_tensor(filt[:, d, 2:4, :], old[:, 0:2, :], sign[:, 0:1], new[:, 2:4, :], ALU.mult,
                                                 ALU.add).then_inc(filt_ready, 1)

            def hyena():
                gain_pre(1, 1)
                at["step"] += 1
                dve.wait_ge(dve_step, at["step"])
                norm(SEQ)
                dve.wait_ge(filt_stored, 32)
                adaln_in(x, SEQ, h_hi, h_lo)
                for n in range(24):
                    b = hy_in.first + n
                    split_ahead(b)
                    d, kind = divmod(n, 3)
                    col = (8, 16, 0)[kind] + d
                    dst = x0[:, d, :] if kind == 2 else short[:, kind, :]
                    dve.wait_ge(mid_ready, n + 1)
                    dve.scalar_tensor_tensor(dst, zp[:, n % 2, 0:SEQ], hy_cols[:, 1, col:col + 1], dst, ALU.mult, ALU.add).then_inc(result_read, 1)
                    at["p"] += 1
                    dve.wait_ge(result_read, BANKS + at["p"])
                    dve.scalar_tensor_tensor(dst, zp[:, n % 2, 2:SEQ + 2], hy_cols[:, 3, col:col + 1], dst, ALU.mult, ALU.add).then_inc(conv_done, 1)
                    if kind == 1:
                        dve.wait_ge(conv_done, n + 1)
                        dve.tensor_tensor(u_t[:, d, :], short[:, 0, :], short[:, 1, :], ALU.mult).then_inc(u_t_ready, 1)

                def gate(n):
                    dve.wait_ge(back_ready, n + 1)
                    if n >= 2:
                        dve.wait_ge(g_ready, n - 1)
                    seq(dve.scalar_tensor_tensor(square[:, n % 2, :], u_t[:, n, :], hy_bias[:, n:n + 1], psum[:, 4 + n % 2, :],
                                                 ALU.mult, ALU.add))
                    dve.tensor_tensor(u_t[:, n, :], square[:, n % 2, :], x0[:, n, :], ALU.mult).then_inc(g_ready, 1)

                for c in range(2):
                    dve.wait_ge(filt_loaded, 16 * (c + 1))
                    dve.wait_ge(uf_ready, 8 * c + 8)
                    if c:
                        dve.wait_ge(back_ready, 4)
                    for n, (i, part) in enumerate(((0, 0), (0, 1), (1, 0))):
                        at["step"] = products(dve, dve_step, at["step"], i, part, term[:, 0, :], term[:, 1, :], yf_ready,
                                              3 * c + n)
                    for t in range(4):
                        gate(4 * c + t)
                for d in range(KT):
                    dve.wait_ge(g_hi_ready, d + 1)
                    dve.tensor_tensor(h_lo[:, d, :], u_t[:, d, :], h_hi[:, d, :].bitcast(F32), ALU.subtract).then_inc(g_split, 1)

            make_filter()
            hyena()
            project(hy_out)
            mixer_post(1)
            ffn(ffns[4], SEQ, 1, 2, 0, x, False, False)

        @block.gpsimd
        def _(pool):
            pool.wait_ge(x_ready, 16)
            pool.dma_start(rope[:], io["rope"][:, 0:2]).then_inc(side_loaded, 16)
            pool.memset(ak[:], 0.0).then_inc(padded, 1)
            pool.memset(rq[:], 0.0).then_inc(padded, 1)
            pool.wait_ge(roped, 5)
            pool.dma_start(rope[:], io["rope"][:, 2:4]).then_inc(side_loaded, 16)
            pool.wait_ge(roped, len(ROTATED))
            pool.wait_ge(block_done, RING + mix_in.first + IN_TILES)
            pool.dma_start(mask[:], io["mask"]).then_inc(side_loaded, 16)
            pool.wait_ge(out_ready, 4)
            pool.dma_start(dist[:], io["dist"]).then_inc(side_loaded, 16)
            pool.wait_ge(x_ready, 40)
            for dst, src in ((pos[:], io["pos"]), (f0[:], io["hy_f0"]), (f12[:, 0, :], io["hy_f1"]), (f12[:, 1, :], io["hy_f2"]),
                             (fb[:], io["hy_fb"]), (f3[0:HID, :], io["hy_f3"])):
                pool.dma_start(dst, src).then_inc(side_loaded, 16)
            pool.dma_start(dft_f[:], io["dft"]).then_inc(side_loaded, 16)
            pool.memset(f3[HID:P, :], 0.0).then_inc(padded, 1)
            pool.memset(hid[HID:P, 0, :], 0.0).then_inc(padded, 1)
            for c in range(2):
                for t in range(POS_TILES):
                    n = c * POS_TILES + t
                    if n >= 2:
                        pool.wait_ge(taps_ready, n - 1)
                    pool.dma_start(taper[:, n % 2, :], io["decay"][t, :, c * 512:c * 512 + 512]).then_inc(taper_landed[n % 2], 16)
                pool.wait_ge(filt_ready, 3 * c + 3)
                pool.dma_start(filt_dram[c], filt[:]).then_inc(filt_stored, 16)
            pool.dma_start(hy_cols[:, 0, :], io["hy_b_in"]).then_inc(side_loaded, 16)
            pool.dma_start(hy_cols[:, 1:4, :], io["hy_short_w"]).then_inc(side_loaded, 16)
            pool.dma_start(hy_cols[:, 4, :], io["hy_short_b"]).then_inc(side_loaded, 16)
            pool.dma_start(hy_bias[:, :], io["hy_bias"]).then_inc(side_loaded, 16)
            pool.memset(zp[:], 0.0).then_inc(padded, 1)
            pool.wait_ge(u_t_ready, KT)
            pool.wait_ge(conv_done, 24)
            pool.dma_start(dft[:], io["dft"]).then_inc(side_loaded, 16)
            pool.dma_start(idft[:], io["idft"]).then_inc(side_loaded, 16)
            step = 0
            for c in range(2):
                pool.wait_ge(block_done, RING + hy_in.first + 24)
                if c:
                    pool.wait_ge(yf_ready, 3)
                    pool.wait_ge(yf_pool_ready, 1)
                pool.wait_ge(filt_stored, 32)
                pool.dma_start(filt[:], filt_dram[c]).then_inc(filt_loaded, 16)
                pool.wait_ge(filt_loaded, 16 * (c + 1))
                pool.wait_ge(uf_ready, 8 * c + 8)
                if c:
                    pool.wait_ge(back_ready, 4)
                step = products(pool, pool_step, step, 1, 1, prod[:].rearrange("p a c -> p (a c)"),
                                full[:].rearrange("p a c -> p (a c)"), yf_pool_ready, c)

    return nc


def constants():
    t = {}
    t["ident"] = np.eye(P, dtype=np.float32)
    half = HEAD // 2
    rot = np.zeros((P, P), np.float32)
    for m in range(P):
        base, r = m // HEAD * HEAD, m % HEAD
        if r < half:
            rot[base + r + half, m] = -1.0
        else:
            rot[base + r - half, m] = 1.0
    t["rot"] = rot
    grid_w = 64
    pos = np.arange(SEQ)
    row, col = (pos // grid_w).astype(np.float32), (pos % grid_w).astype(np.float32)
    nf = HEAD // 4
    inv = (np.float32(10000.0) ** (-np.arange(nf, dtype=np.float32) / nf)).astype(np.float32)
    ang_a = np.concatenate([row[:, None] * inv, col[:, None] * inv], -1).astype(np.float32)
    inv_r = (np.float32(10000.0) ** (-np.linspace(0.0, 1.0, half, dtype=np.float32))).astype(np.float32)
    ang_r = (pos.astype(np.float32)[:, None] * inv_r).astype(np.float32)
    rope = np.zeros((P, 4, SEQ), np.float32)
    for n, ang in enumerate((ang_a, ang_r)):
        rope[:, 2 * n] = np.tile(np.cos(ang).T, (4, 1))
        rope[:, 2 * n + 1] = np.tile(np.sin(ang).T, (4, 1))
    t["rope"] = rope
    q, k = np.arange(P)[:, None], np.arange(3 * P)[None]
    t["mask"] = np.where(np.abs(k - P - q) <= P, 0.0, NEG).astype(np.float32)
    dist = np.arange(G_W)[None] + G_LOW - 3 * P - np.arange(P)[:, None]
    t["dist"] = dist.astype(np.float32)
    two = np.zeros((P, P), np.float32)
    two[:HEAD, :HEAD] = 1.0
    two[HEAD:, HEAD:] = 1.0
    t["head_ones"] = two
    lag = np.arange(-SEQ, SEQ)
    at = np.abs(lag)
    L = SEQ
    bands = (EMB - 1) // 2
    tt = np.append(np.linspace(0.0, 1.0, L, dtype=np.float32), np.float32(1.0))[at]
    w = np.float32(2.0 * math.pi) * at.astype(np.float32) / np.float32(L)
    f = np.linspace(1e-4, bands - 1, bands, dtype=np.float32)
    fw = (f[:, None] * w[None]).astype(np.float32)
    t["pos"] = np.concatenate([tt[None], np.cos(fw), -np.sin(fw)], 0).astype(np.float32)
    lo, hi = math.log(1e-2) / 1.5, math.log(1e-2) / 0.3
    deltas = np.abs(np.linspace(lo, hi, D, dtype=np.float32))
    t["decay"] = np.ascontiguousarray(np.exp(-tt[:, None] * deltas[None]).astype(np.float32).reshape(POS_TILES, P, D))
    n = np.arange(HB)[:, None].astype(np.float64)
    th = math.pi * (2 * np.arange(HB)[None] + 1) / (2 * HB)
    fwd = np.concatenate([np.cos(n * th), -np.sin(n * th)], 1)
    t["dft"] = np.ascontiguousarray(fwd.reshape(2, P, 4, P).transpose(1, 0, 2, 3)).astype(np.float32)
    back = np.concatenate([np.cos(n * th).T, -np.sin(n * th).T], 0) / HB
    t["idft"] = np.ascontiguousarray(back.reshape(4, P, HB).transpose(1, 0, 2)).astype(np.float32)
    sign = np.where(np.arange(P) % 2 == 0, 1.0, -1.0)
    t["sign"] = np.stack([sign, -sign], 1).astype(np.float32)
    return t


def tiles(w):
    K, M = w.shape
    return w.reshape(K // P, P, M // P, P).transpose(2, 1, 0, 3).reshape(M // P, P, K)


def columns(v):
    return np.moveaxis(v.reshape(v.shape[:-1] + (v.shape[-1] // P, P)), -1, 0)


def layout(inp):
    a = {k: np.asarray(v) for k, v in inp.items()}
    o = {}
    o["x"] = a["x"][0].reshape(SEQ, KT, P).transpose(2, 1, 0)
    o["ctx"] = a["ctx"][0].reshape(CTX, KT, P).transpose(2, 1, 0)
    o["c_cols"] = np.stack([columns(a["c"][0]), columns(a["c_ctx"])], -1)
    o["w_mod"] = a["w_mod"].reshape(2, KT, P, NMOD, D).transpose(0, 3, 1, 2, 4)
    o["b_mod"] = columns(a["b_mod"].reshape(2, NMOD, D))
    o["g_pre"] = columns(a["norm_pre"])
    o["g_post"] = columns(a["norm_post"])
    gu, da, db = [], [], []
    for l in range(2):
        for j in range(2):
            pair = np.stack([tiles(a["ffn_gate"][l, j]), tiles(a["ffn_up"][l, j])], 1)
            gu.append(pair.reshape(2 * FT, P, D))
            down = a["ffn_down"][l, j].reshape(FT, P, KT, P).transpose(2, 1, 0, 3)
            n = HALF_TILES[0]
            for out, part, per in ((da, down[:, :, :n], n // 2), (db, down[:, :, n:], (FT - n) // 2)):
                out.append(part.reshape(KT, P, 2, per, P).transpose(0, 2, 1, 3, 4).reshape(2 * KT, P, per * P))
    o["gate_up"], o["down_a"], o["down_b"] = np.stack(gu), np.stack(da), np.stack(db)
    o["mix_in"] = tiles(a["mix_w_in"][0])[ORDER]
    o["mix_out"] = tiles(a["mix_w_out"][0])
    o["hy_in"] = tiles(a["hy_w_in"][0])[[t * KT + d for d in range(KT) for t in (1, 2, 0)]]
    o["hy_out"] = tiles(a["hy_w_out"][0])
    o["sink"] = np.broadcast_to(a["attn_sink"][0][None], (P, HEADS))
    o["ret"] = np.broadcast_to(a["ret_decay"][0].reshape(1, 2 * HEADS), (P, 2 * HEADS))
    o["hy_b_in"] = columns(a["hy_b_in"][0])
    o["hy_short_w"] = columns(a["hy_short_w"][0])
    o["hy_short_b"] = columns(a["hy_short_b"][0])
    o["hy_bias"] = columns(a["hy_bias"][0])
    o["hy_f0"], o["hy_f1"], o["hy_f2"], o["hy_f3"] = a["hy_f0"][0], a["hy_f1"][0], a["hy_f2"][0], a["hy_f3"][0]
    o["hy_fb"] = np.stack([a["hy_fb0"][0], a["hy_fb1"][0], a["hy_fb2"][0], a["hy_freq"][0]], -1)
    o.update(constants())
    return {k: np.ascontiguousarray(v) for k, v in o.items()}


def kernel(**inputs):
    import concourse.bacc as bacc
    from concourse.bass_utils import run_bass_kernel_spmd

    nc = bacc.Bacc("TRN2", target_bir_lowering=False, num_devices=1)
    arrays = layout(inputs)
    io = {k: nc.dram_tensor(f"in_{k}", v.shape, mybir.dt.from_np(v.dtype), kind="ExternalInput").ap()
          for k, v in arrays.items()}
    io["out"] = nc.dram_tensor("out", (P, KT, SEQ), F32, kind="ExternalOutput").ap()
    build(nc, io)
    r = run_bass_kernel_spmd(nc, [{f"in_{k}": v for k, v in arrays.items()}], core_ids=[0])
    got = r.results[0]["out"]
    return np.ascontiguousarray(got.transpose(2, 1, 0).reshape(1, SEQ, D))
```

```python
from contextlib import ExitStack
import math

import numpy as np

import concourse.bass as bass
from concourse import mybir

F32 = mybir.dt.float32
F32R = mybir.dt.float32r
ALU = mybir.AluOpType
ACT = mybir.ActivationFunctionType
AX = mybir.AxisListType

P = 128
D = 1024
KT = D // P
SEQ = 512
CTX = 256
ALL = SEQ + CTX
D_FF = 2816
FT = D_FF // P
HALF_TILES = (12, 10)
HEAD = 64
HEADS = 8
EPS = 1e-6
NEG = -1e30
QK_SCALE = HEAD ** -0.5
RING = 4
BANKS = 4
IN_TILES = 22
MASK_W = 3 * P
G_LOW = -2 * P
G_W = 11 * P
HB = 256
POS_TILES = 8
HID = 64
EMB = 33
NMOD = 9
SHIFT, SCALE, GATE = range(3)

AK, AV, AQ, RV, RK, RQ, RG = [12], [13], [0, 1, 2, 3], [18, 19, 20, 21], [14, 15, 16, 17], [4, 5, 6, 7], [8, 9, 10, 11]
ORDER = AK + AV + AQ + RV + RK + RQ + RG
WITH_CTX = AK + AV + RV + RK
ROTATED = [t for t in ORDER if t in AK + AQ + RK + RQ]
VALUES = AV + RV
KEY_TILES = ALL // P
UNITS = HEADS * (SEQ // P)
ITEMS = HEADS * KEY_TILES
ZERO = 3 * P - G_LOW
LAG = 2
PAIR_ITEMS = 2 * KEY_TILES


def items_of(s):
    return range(min(ITEMS + LAG, ITEMS * s // UNITS), min(ITEMS + LAG, ITEMS * (s + 1) // UNITS))


def step_of(item):
    return next(s for s in range(2 * UNITS) if item in items_of(s))


PAIR_END = [step_of(PAIR_ITEMS * (t + 1) - 1 + LAG) for t in range(HEADS // 2)]
TABLE_AT = [step_of(KEY_TILES * h + 3) for h in range(HEADS)]
INVERTED = 3
MIX_STEPS = PAIR_END[-1] + INVERTED + 4


def sums_before(s):
    return sum(end + 1 < s for end in PAIR_END)


def window(u):
    h, n = divmod(u, SEQ // P)
    lo, hi = max(n - 1, 0), min(n + 2, SEQ // P)
    return h, n, lo, hi, (hi - lo) * P + CTX


def stepped(eng, n, body, layers=(), hidden=None):
    body(0, False)
    if layers:
        hidden(layers[0])
    if n > 2:
        with eng.Fori(1, n - 1) as i:
            body(i, False)
    if len(layers) > 1:
        hidden(layers[1])
    body(n - 1, True)


class Stage:

    def __init__(self, src, blocks, cols, mods=None):
        self.src, self.blocks, self.cols, self.mods = src, blocks, cols, mods
        self.first = 0
        self.layers = ()


def build(nc, io):
    stages = []

    def stage(name, src, blocks, cols, mods=None):
        s = Stage(src, blocks, cols, mods)
        s.first = stages[-1][1].first + stages[-1][1].blocks if stages else 0
        stages.append((name, s))
        return s

    ffns = []
    for which, half0 in [(0, (0, 2)), (0, None)]:
        ffns.append([stage("gu", io["gate_up"][which, 0:24], 24, 1024, half0),
                     stage("dn", io["down_a"][which], 16, 768),
                     stage("gu", io["gate_up"][which, 24:44], 20, 1024),
                     stage("dn", io["down_b"][which], 16, 640)])
    mix_in = stage("mix_in", io["mix_in"], IN_TILES, 1024)
    mix_out = stage("mix_out", io["mix_out"], KT, 1024)
    for which, (half0, half1, down0) in [(1, (None, (1, 0), None)), (2, (None, None, (1, 5)))]:
        ffns.append([stage("gu", io["gate_up"][which, 0:24], 24, 1024, half0),
                     stage("dn", io["down_a"][which], 16, 768, down0),
                     stage("gu", io["gate_up"][which, 24:44], 20, 1024, half1),
                     stage("dn", io["down_b"][which], 16, 640)])
    ffns[3][2].layers, ffns[3][3].layers = (0, 1), (2,)
    hy_in = stage("hy_in", io["hy_in"], 24, 1024)
    hy_out = stage("hy_out", io["hy_out"], KT, 1024)
    ffns.append([stage("gu", io["gate_up"][3, 0:24], 24, 1024),
                 stage("dn", io["down_a"][3], 16, 768),
                 stage("gu", io["gate_up"][3, 24:44], 20, 1024),
                 stage("dn", io["down_b"][3], 16, 640)])
    total_blocks = stages[-1][1].first + stages[-1][1].blocks

    def cols_of(b):
        return next(s.cols for _, s in stages if s.first <= b < s.first + s.blocks)

    with ExitStack() as ctx:
        def sb(name, shape, dt=F32):
            return ctx.enter_context(nc.sbuf_tensor(name, shape, dt))

        def sem(name):
            return ctx.enter_context(nc.semaphore(name))

        with ExitStack() as r:
            h_hi = r.enter_context(nc.sbuf_tensor("h_hi", [P, KT, SEQ], F32R))
            h_lo = r.enter_context(nc.sbuf_tensor("h_lo", [P, KT, SEQ], F32R))
        filt = sb("filt", [P, 3, 4, 512])
        term = sb("term", [P, 2, 1024])
        x = sb("x", [P, KT, SEQ])
        raw = sb("raw", [P, RING, 1024])
        w_hi = sb("w_hi", [P, RING, 1024], F32R)
        w_lo = sb("w_lo", [P, RING, 1024], F32R)
        mod = sb("mod", [P, 2, NMOD, 2, KT])
        gain_in = sb("gain_in", [P, 2, 3, 2, KT])
        gain_out = sb("gain_out", [P, 2, 3, 2, KT])
        b_mod = sb("b_mod", [P, 2, NMOD, KT])
        g_pre = sb("g_pre", [P, 2, 3, KT])
        g_post = sb("g_post", [P, 2, 3, KT])
        c_cols = sb("c_cols", [P, KT, 2])
        c_silu = sb("c_silu", [P, KT, 32])
        ident = sb("ident", [P, P])
        ones = sb("ones", [P, P])
        eps = sb("eps", [P, 1])
        prod = sb("prod", [P, 2, SEQ])
        square = sb("square", [P, 2, SEQ])
        sumsq = sb("sumsq", [P, SEQ])
        rms = sb("rms", [P, 4])
        rinv = sb("rinv", [P, 4])
        full = sb("full", [P, 2, SEQ])
        rinv_wide = full[:, 0, :].rearrange("p (t c) -> p t c", t=4)
        rot = sb("rot", [P, P])
        head_ones = sb("head_ones", [P, P])
        sign = sb("sign", [P, 2])
        sink = sb("sink", [P, HEADS])
        ret = sb("ret", [P, 2 * HEADS])
        log_decay = sb("log_decay", [P, 2 * HEADS])
        ls = sb("ls", [P, 6, 2 * HEADS])
        stats = sb("stats", [P, 2, 8])
        filt_dram = nc.dram_tensor("filt_dram", (2, P, 3, 4, 512), F32).ap()

        scopes = []

        class region:

            def __enter__(self):
                scopes.append(ExitStack())

            def __exit__(self, *_):
                scopes.pop().close()

        def rb(name, shape, dt=F32):
            return scopes[-1].enter_context(nc.sbuf_tensor(name, shape, dt))

        with region():
            cx = rb("cx", [P, KT, CTX])
            y = rb("y", [P, KT, SEQ])
            act_hi = rb("act_hi", [P, 12, SEQ], F32R)
            act_lo = rb("act_lo", [P, 12, SEQ], F32R)
            silu = square
            mod_raw = rb("mod_raw", [P, RING, 1024])
            mod_row = rb("mod_row", [P, 256])
            kept_rinv = rb("kept_rinv", [P, SEQ])
        with region():
            rv = rb("rv", [P, ALL // P, 512])
            rq = rb("rq", [P, HEADS, SEQ])
            rk = rb("rk", [P, 4, ALL])
            av = rb("av", [P, ALL // P, P])
            aq = rb("aq", [P, 4, SEQ])
            ak = rb("ak", [P, 4, ALL])
            with region():
                hc_hi = rb("hc_hi", [P, KT, CTX], F32R)
                hc_lo = rb("hc_lo", [P, KT, CTX], F32R)
                rope = rb("rope", [P, 2, SEQ])
                rg = rb("rg", [P, 4, SEQ])
            with region():
                mask = rb("mask", [P, MASK_W])
                dist = rb("dist", [P, G_W])
                probs = rb("probs", [P, 2, 640])
                probs_t = rb("probs_t", [P, 2, 640])
                corner = rb("corner", [P, P])
                decay = rb("decay", [P, G_W])
                decay_ctx = rb("decay_ctx", [P, 2, SEQ])
        with region():
            hid = rb("hid", [P, 2, 1024])
            rb("kept", [P, 4096])
            f3 = rb("f3", [P, 2 * D])
            taps = rb("taps", [P, POS_TILES, 512])
            taper = rb("taper", [P, 2, 512])
            dft_f = rb("dft_f", [P, 2, 4, P])
            piece = rb("piece", [P, 2, 4, 512])
            pos = rb("pos", [EMB, 1024])
            hid_t = rb("hid_t", [HID, 1024])
            f0 = rb("f0", [EMB, HID])
            f12 = rb("f12", [HID, 2, HID])
            fb = rb("fb", [HID, 4])
        with region():
            x0 = rb("x0", [P, KT, SEQ])
            u_t = rb("u_t", [P, KT, SEQ])
            u = rb("u", [P, 4, D])
            hy_cols = rb("hy_cols", [P, 5, 24])
            hy_bias = rb("hy_bias", [P, KT])
            with region():
                zp = rb("zp", [P, 2, SEQ + 2])
                short = rb("short", [P, 3, SEQ])
            with region():
                dft = rb("dft", [P, 2, 4, P])
                idft = rb("idft", [P, 4, HB])
                spectra = [rb("spectrum0", [P, 2, 4, 512]), rb("spectrum1", [P, 2, 4, 512])]
                u_f = [spectra[0], raw[:].rearrange("p b (m c) -> p (b m) c", c=512).rearrange("p (j m) c -> p j m c", j=2)]
                y_f = [spectra[1], spectra[0]]
        psum = ctx.enter_context(nc.psum_tensor("psum", [P, 8, 512], F32))
        DOWN_BANK, STAT, RBC, MODP, MODT = (4, 3), 5, 5, 6, 7

        raw_landed = [sem(f"raw_landed{i}") for i in range(RING)]
        hi_split, lo_split, block_done, result_read = map(sem, ("hi_split", "lo_split", "block_done", "result_read"))
        silu_ready, act_hi_ready, act_ready = map(sem, ("silu_ready", "act_hi_ready", "act_ready"))
        mod_landed = [sem(f"mod_landed{i}") for i in range(RING)]
        mod_used, mod_row_ready, mod_turned, mod_ready = map(
            sem, ("mod_used", "mod_row_ready", "mod_turned", "mod_ready"))
        loaded, zeroed, c_ready = sem("loaded"), sem("zeroed"), sem("c_ready")
        c_loaded, x_loaded, ctx_loaded = sem("c_loaded"), sem("x_loaded"), sem("ctx_loaded")
        square_ready, square_used = sem("square_ready"), sem("square_used")
        stat_ready, rms_ready, rinv_ready, wide_ready, rbc_ready = map(
            sem, ("stat_ready", "rms_ready", "rinv_ready", "wide_ready", "rbc_ready"))
        norm_ready, full_ready, h_hi_ready, h_ready, x_ready = map(
            sem, ("norm_ready", "full_ready", "h_hi_ready", "h_ready", "x_ready"))
        stored = sem("stored")
        side_loaded, padded, dve_step = sem("side_loaded"), sem("padded"), sem("dve_step")
        z_copied, rot_ready, roped = sem("z_copied"), sem("rot_ready"), sem("roped")
        v_copied, v_turned, v_ready, gate_ready = sem("v_copied"), sem("v_turned"), sem("v_ready"), sem("gate_ready")
        scores_ready, scores_read, exp_ready, probs_ready = map(sem, ("scores_ready", "scores_read", "exp_ready", "probs_ready"))
        probs_turned, probs_t_ready, pv_done = map(sem, ("probs_turned", "probs_t_ready", "pv_done"))
        att_hi_ready, att_out_ready, ret_hi_ready, ret_out_ready = map(
            sem, ("att_hi_ready", "att_out_ready", "ret_hi_ready", "ret_out_ready"))
        ls_in, ls_exp = sem("ls_in"), sem("ls_exp")
        arg_ready, decay_exp = sem("arg_ready"), sem("decay_exp")
        ret_scores, att_ready, ret_done = sem("ret_scores"), sem("att_ready"), sem("ret_done")
        table_ready, rsum_ready = sem("table_ready"), sem("rsum_ready")
        weighed = [square[:, 0, :], square[:, 1, :], sumsq[:, :]]
        silu_g = term[:].rearrange("p a (b c) -> p (a b) c", c=SEQ)
        hid_sum, hid_arg, hid_ready = sem("hid_sum"), sem("hid_arg"), sem("hid_ready")
        taps_sum, taps_ready, taper_landed = sem("taps_sum"), sem("taps_ready"), [sem("taper_landed0"), sem("taper_landed1")]
        piece_sum, piece_ready, filt_ready = map(sem, ("piece_sum", "piece_ready", "filt_ready"))
        filt_stored = [sem(f"filt_stored{d}") for d in range(3)]
        z_ready, mid_ready, conv_done, u_t_ready = map(sem, ("z_ready", "mid_ready", "conv_done", "u_t_ready"))
        u_turned, u_ready, filt_loaded = sem("u_turned"), sem("u_ready"), sem("filt_loaded")
        uf_sum, uf_ready, yf_ready, yf_pool_ready = map(sem, ("uf_sum", "uf_ready", "yf_ready", "yf_pool_ready"))
        back_ready, g_ready, g_hi_ready, g_split = map(sem, ("back_ready", "g_ready", "g_hi_ready", "g_split"))
        pool_step = sem("pool_step")
        osq_ready, osum_ready, orms_ready, oval_ready = map(sem, ("osq_ready", "osum_ready", "orms_ready", "oval_ready"))

        def products(eng, step_sem, step, c, i, part, t0, t1, done, before):
            def flat(v):
                return v.rearrange("p m c -> p (m c)")
            pairs = []
            for j in range(2):
                k_re, k_im = flat(filt[:, i - j + 1, 0:2, :]), flat(filt[:, i - j + 1, 2:4, :])
                u_re, u_im = flat(u_f[c][:, j, 0:2, :]), flat(u_f[c][:, j, 2:4, :])
                pairs += ([(k_re, u_re, ALU.add), (k_im, u_im, ALU.subtract)] if part == 0 else
                          [(k_re, u_im, ALU.add), (k_im, u_re, ALU.add)])
            out = flat(y_f[c][:, i, 2 * part:2 * part + 2, :])
            terms = [out, t0, t1, t0]
            made = [0] * 4
            if before:
                eng.wait_ge(done, before)

            def make(n):
                nonlocal step
                eng.tensor_tensor(terms[n], pairs[n][0], pairs[n][1], ALU.mult).then_inc(step_sem, 1)
                step += 1
                made[n] = step

            def add(n, last=False):
                nonlocal step
                eng.wait_ge(step_sem, step if n > 1 else made[n])
                ins = eng.tensor_tensor(out, out, terms[n], pairs[n][2])
                ins.then_inc(done if last else step_sem, 1)
                step += 0 if last else 1

            make(0)
            make(1)
            make(2)
            add(1)
            eng.wait_ge(step_sem, step)
            make(3)
            add(2)
            add(3, last=True)
            return step

        LOADS = 9
        block = ctx.enter_context(nc.Block())

        @block.sync
        def _(sp):
            sp.dma_start(c_cols[:], io["c_cols"]).then_inc(c_loaded, 16)
            sp.dma_start(x[:], io["x"]).then_inc(x_loaded, 16)

            def load_block(b, rel, first, src):
                slot = (first + rel) % RING
                sp.wait_ge(lo_split, b + 1)
                sp.dma_start(raw[:, slot, 0:src.shape[-1]], src).then_inc(raw_landed[slot], 16)

            def run_stage(s):
                first = s.first

                def step(i, last):
                    for j in range(4):
                        load_block(first + 4 * i + j, j, first, s.src[4 * i + j])
                if s.blocks % 4 == 0:
                    stepped(sp, s.blocks // 4, step)
                else:
                    for b in range(s.blocks):
                        load_block(first + b, b, first, s.src[b])

            sp.wait_ge(mod_used, RING + 8)
            for ss in ffns[0:2]:
                for s in ss:
                    run_stage(s)
            run_stage(mix_in)
            run_stage(mix_out)
            for ss in ffns[2:4]:
                for s in ss:
                    run_stage(s)
            run_stage(hy_in)
            sp.wait_ge(yf_ready, 6)
            sp.wait_ge(yf_pool_ready, 2)
            run_stage(hy_out)
            for s in ffns[4]:
                run_stage(s)
            for d in range(KT):
                sp.wait_ge(x_ready, 48 + d + 1)
                sp.dma_start(io["out"][:, d], x[:, d, :]).then_inc(stored, 16)
            sp.wait_ge(stored, 16 * KT)

        @block.tensor
        def _(pe):
            at = {"p": 0, "f": 0, "group": 0, "norm": 0, "h": 0}
            pe.sem_inc(block_done, RING)
            pe.sem_inc(mod_used, RING)

            def three(out, w, cols, hi, lo, start, stop):
                slot, c = w
                pe.matmul(out, w_hi[:, slot, c:c + P], hi, start=start, stop=False)
                pe.matmul(out, w_hi[:, slot, c:c + P], lo, start=False, stop=False)
                return pe.matmul(out, w_lo[:, slot, c:c + P], hi, start=False, stop=stop)

            def mod_units(g, ks):
                for k in ks:
                    pe.wait_ge(mod_landed[k % RING], 16 * (2 * g + k // RING + 1))
                    for j in range(4):
                        ins = pe.matmul(psum[32 * j:32 * j + 32, MODP, 0:256], c_silu[:, k, :],
                                        mod_raw[:, k % RING, 256 * j:256 * j + 256],
                                        start=(k == 0), stop=(k == 7), tile_position=(0, 32 * j))
                    ins.then_inc(mod_used, 1)

            def mod_turn(g):
                pe.wait_ge(mod_row_ready, g + 1)
                for half in range(2):
                    ins = pe.transpose(psum[:, MODT, half * P:half * P + P], mod_row[:, half * P:half * P + P], ident[:, :])
                ins.then_inc(mod_turned, 1)

            def hidden(layer):
                if layer == 0:
                    pe.wait_ge(side_loaded, 16 * 9)
                    pe.wait_ge(mod_ready, 2 * NMOD)
                else:
                    pe.wait_ge(hid_ready, layer)
                for c in range(2):
                    lhs = f0[:, :] if layer == 0 else f12[:, layer - 1, :]
                    rhs = pos[:, c * 512:c * 512 + 512] if layer == 0 else hid[0:HID, 0, c * 512:c * 512 + 512]
                    ins = pe.matmul(psum[0:HID, 6 + c, :], lhs, rhs, start=True, stop=True)
                ins.then_inc(hid_sum, 1)

            def gate_up(s, T):
                b0, p0, g0 = s.first, at["p"], at["group"]
                h0 = at["h"]

                def step(i, last):
                    for j in range(4):
                        pe.wait_ge(lo_split, RING + b0 + 4 * i + j + 1)
                        pe.wait_ge(result_read, p0 + 4 * i + j + 1)
                        bank = (p0 + j) % 4
                        slot = (b0 + j) % RING
                        for k in range(KT):
                            if j == 0:
                                pe.wait_ge(h_ready, h0 - KT + k + 1)
                            ins = three(psum[:, bank, 0:T], (slot, k * P), P, h_hi[:, k, 0:T], h_lo[:, k, 0:T],
                                        k == 0, k == KT - 1)
                        ins.then_inc(block_done, 1)
                        if s.mods:
                            mod_units(g0 + i, ((0, 1, 2), (3, 4, 5), (6, 7), ())[j])
                    if s.mods:
                        mod_turn(g0 + i)
                stepped(pe, s.blocks // 4, step, s.layers, hidden)
                at["p"] += s.blocks
                at["f"] += s.blocks // 2
                if s.mods:
                    at["group"] += s.blocks // 4

            def down(s, T, tiles):
                b0, p0, g0, f0 = s.first, at["p"], at["group"], at["f"] - tiles
                per = tiles // 2

                def step(i, last):
                    for dd in range(2):
                        bank = DOWN_BANK[dd]
                        if dd or not isinstance(i, int) or i:
                            pe.wait_ge(result_read, BANKS + p0 + 2 * i + dd - 1)
                        for half in range(2):
                            j = 2 * dd + half
                            slot = (b0 + j) % RING
                            pe.wait_ge(lo_split, RING + b0 + 4 * i + j + 1)
                            for t in range(per):
                                f = half * per + t
                                if dd == 0 and (f == 0 or f == tiles - 1):
                                    pe.wait_ge(act_ready, f0 + (tiles - 1 if f == 0 else tiles))
                                ins = three(psum[:, bank, 0:T], (slot, t * P), P, act_hi[:, f, 0:T], act_lo[:, f, 0:T],
                                            f == 0, f == tiles - 1)
                            ins.then_inc(block_done, 1)
                            if s.mods:
                                mod_units(g0 + i, ((0, 1, 2), (3, 4, 5), (6, 7), ())[j])
                    if s.mods:
                        mod_turn(g0 + i)
                stepped(pe, s.blocks // 4, step, s.layers, hidden)
                at["p"] += s.blocks // 2
                if s.mods:
                    at["group"] += s.blocks // 4

            def norm(T, fill=False):
                n = at["norm"]
                nt = T // P
                pe.wait_ge(square_used, KT * (n + 1))
                for t in range(nt):
                    ins = pe.matmul(psum[:, STAT, t:t + 1], sumsq[:, t * P:t * P + P], ones[:, 0:1], start=True, stop=True)
                ins.then_inc(stat_ready, 1)
                if fill:
                    mod_units(at["group"], list(range(8)))
                pe.wait_ge(wide_ready, n + 1)
                for t in range(nt):
                    ins = pe.matmul(psum[:, RBC, t * P:t * P + P], rinv_wide[:, t, :], ident[:, :], start=True, stop=True)
                ins.then_inc(rbc_ready, 1)
                at["norm"] += 1
                if fill:
                    mod_turn(at["group"])
                    at["group"] += 1

            def ffn(ss, T):
                if ss not in ffns[0:2]:
                    norm(T)
                at["h"] += KT
                gate_up(ss[0], T)
                if ss is ffns[1]:
                    norm(SEQ)
                down(ss[1], T, HALF_TILES[0])
                gate_up(ss[2], T)
                down(ss[3], T, HALF_TILES[1])
                norm(T, fill=ss is ffns[0])

            pe.wait_ge(zeroed, 3)
            pe.wait_ge(c_ready, 1)
            mod_units(0, list(range(8)))
            pe.wait_ge(loaded, 16 * LOADS)
            norm(CTX)
            mod_turn(0)
            mod_units(1, list(range(8)))
            norm(SEQ)
            mod_turn(1)
            at["group"] += 2
            ffn(ffns[0], SEQ)
            ffn(ffns[1], CTX)

            def mixer_in():
                norm(CTX)
                at["h"] += 2 * KT
                rotated = values = 0

                def after(tile):
                    nonlocal rotated, values
                    if tile in ROTATED:
                        pe.wait_ge(z_copied, rotated + 1)
                        if rotated >= 2:
                            pe.wait_ge(roped, rotated - 1)
                        pe.matmul(psum[:, 4 + rotated % 2, :], rot[:, :], full[:, rotated % 2, :],
                                  start=True, stop=True).then_inc(rot_ready, 1)
                        rotated += 1
                    if tile in VALUES:
                        pe.wait_ge(v_copied, values + 1)
                        if values:
                            pe.wait_ge(v_ready, values)
                        for t in range(KEY_TILES):
                            src = sumsq[:, t * P:t * P + P] if t < 4 else prod[:, 1, (t - 4) * P:(t - 3) * P]
                            ins = pe.transpose(psum[:, 6 + t // 4, t % 4 * P:t % 4 * P + P], src, ident[:, :])
                        ins.then_inc(v_turned, 1)
                        values += 1

                for n, tile in enumerate(ORDER):
                    b = mix_in.first + n
                    pe.wait_ge(lo_split, RING + b + 1)
                    for T, hi, lo in ((SEQ, h_hi, h_lo), (CTX, hc_hi, hc_lo))[:2 if tile in WITH_CTX else 1]:
                        pe.wait_ge(result_read, at["p"] + 1)
                        for k in range(KT):
                            if n == 0:
                                pe.wait_ge(h_ready, at["h"] - (KT if T == SEQ else 2 * KT) + k + 1)
                            ins = three(psum[:, at["p"] % 4, 0:T], (b % RING, k * P), P, hi[:, k, 0:T], lo[:, k, 0:T],
                                        k == 0, k == KT - 1)
                        at["p"] += 1
                    ins.then_inc(block_done, 1)
                    if n:
                        after(ORDER[n - 1])
                after(ORDER[-1])

            def attention_retention():
                pe.wait_ge(roped, len(ROTATED))
                pe.wait_ge(v_ready, len(VALUES))
                pe.wait_ge(result_read, at["p"] + BANKS)
                ring = []

                def score(u):
                    h, n, lo, hi, _ = window(u)
                    k = ak[:, 2 * (h // 4) + h % 2, :]
                    q = aq[:, h // 2, n * P:n * P + P]
                    if u >= 2:
                        pe.wait_ge(probs_t_ready, u - 1)
                    a = 2 * (u % 2)
                    pe.matmul(psum[:, a, 0:(hi - lo) * P], q, k[:, lo * P:hi * P], start=True, stop=True)
                    pe.matmul(psum[:, a + 1, 0:CTX], q, k[:, SEQ:ALL], start=True, stop=True).then_inc(scores_ready, 1)

                def turn(u):
                    a, w = 2 * (u % 2), window(u)[4] // P
                    pe.wait_ge(probs_ready, u + 1)
                    for t in range(w):
                        ins = pe.transpose(psum[:, a + t // 4, t % 4 * P:t % 4 * P + P], probs[:, u % 2, t * P:t * P + P],
                                           ident[:, :])
                    ins.then_inc(probs_turned, 1)

                def pv(u):
                    h, n, lo, hi, _ = window(u)
                    keys = list(range(lo, hi)) + [4, 5]
                    r0 = HEAD * (h % 2)
                    pe.wait_ge(probs_t_ready, u + 1)
                    if u % 8 == 0 and u:
                        pe.wait_ge(att_out_ready, u // 8)
                    for t, key in enumerate(keys):
                        ins = pe.matmul(psum[r0:r0 + HEAD, 4, n * P:n * P + P],
                                        av[:, key, HEAD * (h // 4):HEAD * (h // 4) + HEAD], probs_t[:, u % 2, t * P:t * P + P],
                                        start=(t == 0), stop=(t == len(keys) - 1))
                    ins.then_inc(pv_done, 1)

                def ring_bank():
                    if len(ring) >= 2:
                        pe.wait_ge(*ring[-2])
                    return 5 + len(ring) % 2

                def ret_score(i):
                    h, j = divmod(i, KEY_TILES)
                    pe.matmul(psum[:, ring_bank(), :], rk[:, h // 2, j * P:j * P + P], rq[:, h, :],
                              start=True, stop=True).then_inc(ret_scores, 1)
                    ring.append((att_ready, i + 1))

                def ret_value(i):
                    h, j = divmod(i, KEY_TILES)
                    r0 = HEAD * (h % 2)
                    pe.wait_ge(att_ready, i + 1)
                    if i and i % PAIR_ITEMS == 0:
                        pe.wait_ge(osq_ready, i // PAIR_ITEMS)
                    pe.matmul(psum[r0:r0 + HEAD, 7, :], rv[:, j, h * HEAD:h * HEAD + HEAD], weighed[i % 3],
                              start=(j == 0), stop=(j == KEY_TILES - 1)).then_inc(ret_done, 1)

                def sums(t):
                    pe.wait_ge(osq_ready, t + 1)
                    pe.matmul(psum[:, ring_bank(), :], head_ones[:, :], full[:, 0, :], start=True, stop=True).then_inc(osum_ready, 1)
                    ring.append((orms_ready, t + 1))

                for s in range(MIX_STEPS):
                    if s < UNITS:
                        score(s)
                    for i in items_of(s):
                        if i < ITEMS:
                            ret_score(i)
                        if i >= LAG:
                            ret_value(i - LAG)
                    if 1 <= s <= UNITS:
                        turn(s - 1)
                    if 2 <= s <= UNITS + 1:
                        pv(s - 2)
                    if s - 1 in PAIR_END:
                        sums(PAIR_END.index(s - 1))

            def project(s, ready):
                for d in range(s.blocks):
                    b = s.first + d
                    pe.wait_ge(lo_split, RING + b + 1)
                    pe.wait_ge(result_read, at["p"] + 1)
                    for k in range(KT):
                        if d == 0:
                            ready(k)
                        ins = three(psum[:, at["p"] % 4, :], (b % RING, k * P), P, h_hi[:, k, :], h_lo[:, k, :],
                                    k == 0, k == KT - 1)
                    ins.then_inc(block_done, 1)
                    at["p"] += 1

            mixer_in()
            attention_retention()
            project(mix_out, lambda k: pe.wait_ge(att_out_ready, k + 1) if k < 4 else pe.wait_ge(ret_out_ready, k - 3))
            norm(SEQ)

            ffn(ffns[2], SEQ)
            ffn(ffns[3], SEQ)

            def make_filter():
                pe.wait_ge(side_loaded, 16 * 11)
                pe.wait_ge(padded, 4)
                pe.wait_ge(result_read, at["p"] + BANKS)
                pe.wait_ge(hid_ready, 3)
                for c in range(2):
                    for t in range(POS_TILES):
                        n = c * POS_TILES + t
                        if n >= 2:
                            pe.wait_ge(taps_ready, n - 1)
                        col = (D if t < 4 else 0) + c * 512
                        pe.matmul(psum[:, 6 + n % 2, :], hid[:, 0, t * P:t * P + P], f3[:, col:col + 512],
                                  start=True, stop=True).then_inc(taps_sum, 1)
                    for a in range(4):
                        n = 4 * c + a
                        pe.wait_ge(taps_ready, POS_TILES * c + 2 * a + 2)
                        if n:
                            pe.wait_ge(piece_ready, n)
                        for m in range(4):
                            for k in range(2):
                                ins = pe.matmul(psum[:, m, :], dft_f[:, k, m, :], taps[:, 2 * a + k, :], start=(k == 0), stop=(k == 1))
                        ins.then_inc(piece_sum, 1)

            def hyena():
                norm(SEQ)
                at["h"] += KT

                def turn(d):
                    pe.wait_ge(u_t_ready, d + 1)
                    if d >= 2:
                        pe.wait_ge(u_ready, d - 1)
                    for t in range(4):
                        ins = pe.transpose(psum[:, 6 + d % 2, t * P:t * P + P], u_t[:, d, t * P:t * P + P], ident[:, :])
                    ins.then_inc(u_turned, 1)

                for n in range(24):
                    b = hy_in.first + n
                    pe.wait_ge(lo_split, RING + b + 1)
                    pe.wait_ge(result_read, at["p"] + 1)
                    for k in range(KT):
                        if n == 0:
                            pe.wait_ge(h_ready, at["h"] - KT + k + 1)
                        ins = three(psum[:, at["p"] % 4, :], (b % RING, k * P), P, h_hi[:, k, :], h_lo[:, k, :],
                                    k == 0, k == KT - 1)
                    ins.then_inc(block_done, 1)
                    at["p"] += 1
                    if n % 3 == 0 and n:
                        turn(n // 3 - 1)
                turn(7)
                pe.wait_ge(side_loaded, 16 * 17)
                pe.wait_ge(u_ready, KT)
                pe.wait_ge(result_read, at["p"] + BANKS)
                for c in range(2):
                    for j in range(2):
                        for m in range(4):
                            n = 8 * c + 4 * j + m
                            if n >= 4:
                                pe.wait_ge(uf_ready, n - 3)
                            for k in range(2):
                                ins = pe.matmul(psum[:, n % 4, :], dft[:, k, m, :], u[:, 2 * j + k, c * 512:c * 512 + 512],
                                                start=(k == 0), stop=(k == 1))
                            ins.then_inc(uf_sum, 1)
                for c in range(2):
                    pe.wait_ge(yf_ready, 3 * c + 3)
                    pe.wait_ge(yf_pool_ready, c + 1)
                    for t in range(4):
                        n = 4 * c + t
                        if n >= 2:
                            pe.wait_ge(g_ready, n - 1)
                        for i in range(2):
                            for m in range(4):
                                ins = pe.matmul(psum[:, 4 + n % 2, i * HB:i * HB + HB], y_f[c][:, i, m, t * P:t * P + P], idft[:, m, :],
                                                start=(m == 0), stop=(m == 3))
                        ins.then_inc(back_ready, 1)

            make_filter()
            hyena()
            project(hy_out, lambda k: pe.wait_ge(g_split, k + 1))
            norm(SEQ)
            ffn(ffns[4], SEQ)

        @block.scalar
        def _(act):
            at = {"p": 0, "f": 0, "norm": 0, "xr": 0, "pre": 0}

            def split_hi(b0, i, cols):
                slot = b0 % RING
                act.wait_ge(raw_landed[slot], 16 * (i + b0 // RING + 1))
                act.wait_ge(block_done, b0 + 4 * i + 1)
                act.activation(w_hi[:, slot, 0:cols], raw[:, slot, 0:cols], ACT.Copy).then_inc(hi_split, 1)

            def ahead(s, i, rel, last):
                if last and s.first + 4 * i + rel >= total_blocks:
                    return
                cols = cols_of(s.first + 4 * i + rel) if last else s.cols
                split_hi(s.first + rel, i, cols)

            def hidden(layer):
                act.wait_ge(hid_arg, layer + 1)
                act.activation(hid[0:HID, 0, :], hid_t[:, :], ACT.Sin).then_inc(hid_ready, 1)

            def gate_up(s, T):
                b0, p0, f0 = s.first, at["p"], at["f"]

                def step(i, last):
                    for j in range(2):
                        ahead(s, i, 2 * j + 2, last)
                        ahead(s, i, 2 * j + 3, last)
                        bank = (p0 + 2 * j) % 4
                        act.wait_ge(block_done, RING + b0 + 4 * i + 2 * j + 1)
                        act.activation(silu[:, j, 0:T], psum[:, bank, 0:T], ACT.Silu).then_inc(silu_ready, 1)
                        act.wait_ge(result_read, BANKS + p0 + 4 * i + 2 * j + 2)
                        act.activation(act_hi[:, bass.ds(2 * i + j, 1), 0:T], prod[:, j:j + 1, 0:T],
                                       ACT.Copy).then_inc(act_hi_ready, 1)
                stepped(act, s.blocks // 4, step, s.layers, hidden)
                at["p"] += s.blocks
                at["f"] += s.blocks // 2

            def down(s, T, final):
                n0, p0 = KT * at["norm"], at["p"]

                def step(i, last):
                    for dd in range(2):
                        ahead(s, i, 2 * dd + 2, last)
                        ahead(s, i, 2 * dd + 3, last)
                        if final:
                            act.wait_ge(result_read, BANKS + p0 + 2 * i + dd + 1)
                            act.wait_ge(square_used, n0 + 2 * i + dd - 1)
                            act.activation(square[:, dd:dd + 1, 0:T], y[:, bass.ds(2 * i + dd, 1), 0:T],
                                           ACT.Square).then_inc(square_ready, 1)
                stepped(act, s.blocks // 4, step, s.layers, hidden)
                at["p"] += s.blocks // 2

            def copy_piece(n):
                act.wait_ge(piece_sum, n + 1)
                if n >= 2:
                    act.wait_ge(filt_ready, 3 * ((n - 1) // 4) + (n - 1) % 4)
                act.activation(piece[:, n % 2], psum[:, 0:4, :], ACT.Copy).then_inc(piece_ready, 1)

            def square_x(src, T, base, piece_at=()):
                n0 = KT * at["norm"]
                for d in range(KT):
                    if base is not None:
                        act.wait_ge(x_ready, base + d + 1)
                    if n0 + d >= 2:
                        act.wait_ge(square_used, n0 + d - 1)
                    act.activation(square[:, d % 2, 0:T], src[:, d, 0:T], ACT.Square).then_inc(square_ready, 1)
                    if d in piece_at:
                        copy_piece(piece_at.index(d))

            def norm(T):
                n = at["norm"]
                act.wait_ge(stat_ready, n + 1)
                act.activation(rms[:, 0:T // P], psum[:, STAT, 0:T // P], ACT.Sqrt, bias=eps[:, 0:1],
                               scale=1.0 / D).then_inc(rms_ready, 1)
                at["norm"] += 1

            def adaln_in(T, layer, i, who, hi):
                c0 = KT * at["pre"]
                for d in range(KT):
                    act.wait_ge(norm_ready, c0 + d + 1)
                    if d >= 2:
                        act.wait_ge(h_ready, c0 + d - 1)
                    act.activation(full[:, d % 2, 0:T], prod[:, d % 2, 0:T], ACT.Identity,
                                   bias=mod[:, layer, 3 * i, who, d:d + 1],
                                   scale=gain_in[:, layer, i, who, d:d + 1]).then_inc(full_ready, 1)
                    act.wait_ge(full_ready, c0 + d + 1)
                    act.activation(hi[:, d, 0:T], full[:, d % 2, 0:T], ACT.Copy).then_inc(h_hi_ready, 1)
                at["pre"] += 1

            def ffn(ss, T, layer, i, who, src, chain):
                if ss not in ffns[0:2]:
                    norm(T)
                if ss is not ffns[1]:
                    adaln_in(T, layer, i, who, h_hi)
                gate_up(ss[0], T)
                if ss is ffns[1]:
                    norm(SEQ)
                down(ss[1], T, False)
                gate_up(ss[2], T)
                down(ss[3], T, True)
                norm(T)
                if ss is ffns[0]:
                    adaln_in(CTX, 0, 0, 1, h_hi)
                if chain:
                    square_x(src, T, at["xr"], (3, 7) if ss is ffns[3] else ())
                at["xr"] += KT

            act.dma_start(cx[:], io["ctx"]).then_inc(ctx_loaded, 16)
            for dst, src in ((ident, "ident"), (b_mod, "b_mod"), (g_pre, "g_pre"), (g_post, "g_post"), (rot, "rot"),
                             (head_ones, "head_ones"), (sign, "sign"), (sink, "sink"), (ret, "ret")):
                act.dma_start(dst[:], io[src]).then_inc(loaded, 16)
            act.wait_ge(zeroed, 3)
            act.wait_ge(c_loaded, 16)
            act.activation(c_silu[:, :, 0:2], c_cols[:], ACT.Silu).then_inc(c_ready, 1)
            act.wait_ge(loaded, 16 * LOADS)
            act.wait_ge(ctx_loaded, 16)
            square_x(cx, CTX, None)
            norm(CTX)
            act.wait_ge(x_loaded, 16)
            square_x(x, SEQ, None)
            norm(SEQ)
            for b in range(2):
                split_hi(b, 0, 1024)
            ffn(ffns[0], SEQ, 0, 0, 0, x, True)
            act.wait_ge(square_used, KT * (at["norm"] + 1))
            ffn(ffns[1], CTX, 0, 0, 1, cx, True)

            def split_ahead(b):
                if b + 2 < total_blocks:
                    split_hi(b + 2, 0, cols_of(b + 2))

            def mixer_in():
                norm(CTX)
                adaln_in(CTX, 0, 1, 1, hc_hi)
                adaln_in(SEQ, 0, 1, 0, h_hi)
                rotated = values = 0
                p = at["p"]

                def turned():
                    nonlocal values
                    act.wait_ge(v_turned, values + 1)
                    dst = av if values == 0 else rv[:, :, (values - 1) * P:values * P]
                    act.activation(dst[:, 0:4, :], psum[:, 6, :].rearrange("p (t c) -> p t c", t=4), ACT.Copy)
                    act.activation(dst[:, 4:6, :], psum[:, 7, 0:CTX].rearrange("p (t c) -> p t c", t=2),
                                   ACT.Copy).then_inc(v_ready, 1)
                    values += 1

                for n, tile in enumerate(ORDER):
                    b = mix_in.first + n
                    split_ahead(b)
                    if tile == RQ[0]:
                        act.wait_ge(ls_in, 1)
                        act.activation(ls[:, 1, :], ls[:, 0, :], ACT.Exp, scale=-1.0).then_inc(ls_exp, 1)
                    if n and ORDER[n - 1] in VALUES:
                        turned()
                    if tile in ROTATED:
                        act.wait_ge(block_done, RING + b + 1)
                        if rotated >= 2:
                            act.wait_ge(rot_ready, rotated - 1)
                        act.activation(full[:, rotated % 2, :], psum[:, p % 4, :], ACT.Copy).then_inc(z_copied, 1)
                        rotated += 1
                    p += 2 if tile in WITH_CTX else 1
                at["p"] = p
                act.wait_ge(gate_ready, 1)
                act.wait_ge(block_done, RING + mix_in.first + IN_TILES)
                act.activation(silu_g, rg[:], ACT.Silu).then_inc(gate_ready, 1)

            def attention_retention():
                def exps(u):
                    w, i = window(u)[4], u % 2
                    act.wait_ge(scores_read, u + 1)
                    act.activation(probs[:, i, 0:w], probs[:, i, 0:w], ACT.Exp, bias=stats[:, i, 1:2],
                                   accum_out=stats[:, i, 2:3])
                    act.activation(stats[:, i, 3:4], sink[:, u // 4:u // 4 + 1], ACT.Exp,
                                   bias=stats[:, i, 1:2]).then_inc(exp_ready, 1)

                def normalize(u):
                    w, i = window(u)[4], u % 2
                    act.wait_ge(rsum_ready, u + 1)
                    act.activation(probs[:, i, 0:w], probs[:, i, 0:w], ACT.Copy, scale=stats[:, i, 5:6]).then_inc(probs_ready, 1)

                def copy_out(u):
                    a, w = 2 * (u % 2), window(u)[4]
                    act.wait_ge(probs_turned, u + 1)
                    if u >= 2:
                        act.wait_ge(pv_done, u - 1)
                    flat = psum[:, a:a + 2, :].rearrange("p b c -> p (b c)")
                    act.activation(probs_t[:, u % 2, 0:w], flat[:, 0:w], ACT.Copy).then_inc(probs_t_ready, 1)

                def att_out(t):
                    act.wait_ge(pv_done, 8 * t + 8)
                    act.activation(h_hi[:, t, :], psum[:, 4, :], ACT.Copy).then_inc(att_hi_ready, 1)

                def table(h):
                    act.wait_ge(arg_ready, h + 1)
                    if h:
                        act.wait_ge(att_ready, KEY_TILES * (h - 1) + 4)
                        act.wait_ge(table_ready, 2 * h)
                    act.activation(decay[:, 0:ZERO], dist[:, 0:ZERO], ACT.Exp, scale=log_decay[:, HEADS + h:HEADS + h + 1])
                    act.activation(decay[:, ZERO + P:G_W], dist[:, ZERO + P:G_W], ACT.Exp, scale=log_decay[:, h:h + 1])
                    act.activation(decay[:, ZERO:ZERO + P], corner[:, :], ACT.Exp).then_inc(decay_exp, 1)

                def squares(t):
                    act.wait_ge(ret_done, PAIR_ITEMS * (t + 1))
                    if t:
                        act.wait_ge(ret_out_ready, t)
                    act.activation(prod[:, 0, :], psum[:, 7, :], ACT.Copy)
                    act.activation(full[:, 0, :], psum[:, 7, :], ACT.Square).then_inc(osq_ready, 1)

                def root(t, bank):
                    act.wait_ge(osum_ready, t + 1)
                    act.activation(full[:, 1, :], psum[:, bank, :], ACT.Sqrt, bias=eps[:, 0:1],
                                   scale=1.0 / HEAD).then_inc(orms_ready, 1)

                def ret_out(t):
                    act.wait_ge(oval_ready, t + 1)
                    act.activation(h_hi[:, 4 + t, :], full[:, 0, :], ACT.Copy).then_inc(ret_hi_ready, 1)

                act.wait_ge(side_loaded, 64)
                act.wait_ge(gate_ready, 2)
                table(0)
                for s in range(MIX_STEPS):
                    if s in PAIR_END:
                        squares(PAIR_END.index(s))
                    if s >= 10 and (s - 10) % 8 == 0 and s <= UNITS + 2:
                        att_out((s - 10) // 8)
                    if 1 <= s <= UNITS:
                        normalize(s - 1)
                    if s < UNITS:
                        exps(s)
                    if 1 <= s <= UNITS:
                        copy_out(s - 1)
                    if s in TABLE_AT[:-1]:
                        table(TABLE_AT.index(s) + 1)
                    if s - 1 in PAIR_END:
                        t = PAIR_END.index(s - 1)
                        root(t, 5 + (min(ITEMS, items_of(s).stop) + t) % 2)
                    if s - INVERTED - 2 in PAIR_END:
                        ret_out(PAIR_END.index(s - INVERTED - 2))

            def project(s):
                n0, p0 = KT * at["norm"], at["p"]
                for d in range(KT):
                    split_ahead(s.first + d)
                    act.wait_ge(result_read, BANKS + p0 + d + 1)
                    act.wait_ge(square_used, n0 + d - 1)
                    act.activation(square[:, d % 2, :], y[:, d, :], ACT.Square).then_inc(square_ready, 1)
                at["p"] += KT

            mixer_in()
            attention_retention()
            project(mix_out)
            norm(SEQ)
            square_x(x, SEQ, at["xr"])
            at["xr"] += KT

            ffn(ffns[2], SEQ, 0, 2, 0, x, True)
            ffn(ffns[3], SEQ, 1, 0, 0, x, True)

            def make_filter():
                for n in range(2, 8):
                    copy_piece(n)

            def hyena():
                norm(SEQ)
                adaln_in(SEQ, 1, 1, 0, h_hi)
                act.wait_ge(side_loaded, 16 * 15)
                act.wait_ge(padded, 5)

                def turned(d):
                    act.wait_ge(u_turned, d + 1)
                    act.activation(u[:, :, d * P:d * P + P], psum[:, 6 + d % 2, :].rearrange("p (t c) -> p t c", t=4),
                                   ACT.Copy).then_inc(u_ready, 1)

                for n in range(24):
                    b = hy_in.first + n
                    if n < 22:
                        split_ahead(b)
                    d, kind = divmod(n, 3)
                    col = (8, 16, 0)[kind] + d
                    act.wait_ge(block_done, RING + b + 1)
                    if n >= 2:
                        act.wait_ge(conv_done, n - 1)
                    act.activation(zp[:, n % 2, 1:SEQ + 1], psum[:, at["p"] % 4, :], ACT.Identity,
                                   bias=hy_cols[:, 0, col:col + 1]).then_inc(z_ready, 1)
                    at["p"] += 1
                    act.wait_ge(z_ready, n + 1)
                    if kind == 0 and d:
                        act.wait_ge(u_t_ready, d)
                    dst = x0[:, d, :] if kind == 2 else short[:, kind, :]
                    act.activation(dst, zp[:, n % 2, 1:SEQ + 1], ACT.Identity, bias=hy_cols[:, 4, col:col + 1],
                                   scale=hy_cols[:, 2, col:col + 1]).then_inc(mid_ready, 1)
                    if n % 3 == 1 and n > 3:
                        turned(n // 3 - 1)
                turned(7)
                for c in range(2):
                    if c:
                        act.wait_ge(lo_split, RING + hy_out.first)
                    for k in range(8):
                        act.wait_ge(uf_sum, 8 * c + k + 1)
                        act.activation(u_f[c][:, k // 4, k % 4, :], psum[:, k % 4, :], ACT.Copy).then_inc(uf_ready, 1)
                for d in range(KT):
                    if d == 4:
                        split_hi(hy_out.first, 0, 1024)
                        split_hi(hy_out.first + 1, 0, 1024)
                    act.wait_ge(g_ready, d + 1)
                    if d == 0:
                        act.wait_ge(yf_ready, 6)
                        act.wait_ge(yf_pool_ready, 2)
                    act.activation(h_hi[:, d, :], u_t[:, d, :], ACT.Copy).then_inc(g_hi_ready, 1)

            make_filter()
            hyena()
            project(hy_out)
            norm(SEQ)
            square_x(x, SEQ, at["xr"])
            at["xr"] += KT
            ffn(ffns[4], SEQ, 1, 2, 0, x, False)

        @block.vector
        def _(dve):
            at = {"p": 0, "f": 0, "norm": 0, "xr": 0, "pre": 0, "group": 0, "step": 0, "z": 3}
            dve.memset(ones[:, :], 1.0).then_inc(zeroed, 1)
            dve.memset(eps[:, :], EPS).then_inc(zeroed, 1)
            dve.memset(c_silu[:], 0.0).then_inc(zeroed, 1)
            dve.sem_inc(lo_split, RING)
            dve.sem_inc(result_read, BANKS)

            def split_lo(b0, i, cols):
                slot = b0 % RING
                dve.wait_ge(hi_split, b0 + 4 * i + 1)
                ins = dve.tensor_tensor(w_lo[:, slot, 0:cols], raw[:, slot, 0:cols], w_hi[:, slot, 0:cols].bitcast(F32),
                                        ALU.subtract)
                ins.then_inc(lo_split, 1)

            def ahead(s, i, rel, last):
                if last and s.first + 4 * i + rel >= total_blocks:
                    return
                cols = cols_of(s.first + 4 * i + rel) if last else s.cols
                split_lo(s.first + rel, i, cols)

            def mod_copy(g):
                dve.wait_ge(mod_used, RING + 8 * g + 8)
                dve.tensor_copy(mod_row[:, :], psum[:, MODP, 0:256]).then_inc(mod_row_ready, 1)

            def mod_finish(g, layer, v):
                dve.wait_ge(mod_turned, g + 1)
                turned = psum[:, MODT, 0:256].rearrange("p (h j c) -> p c j h", h=2, j=4)
                for who in range(2):
                    dst = mod[:, layer, bass.ds(v, 1), who, :].rearrange("p o (j h) -> p (o j) h", h=2)
                    bias = b_mod[:, layer, bass.ds(v, 1), :].rearrange("p o (j h) -> p (o j) h", h=2)
                    ins = dve.tensor_tensor(dst, turned[:, who], bias, ALU.add)
                ins.then_inc(mod_ready, 1)

            def make_taps(c):
                for t in range(POS_TILES):
                    n = c * POS_TILES + t
                    dve.wait_ge(taps_sum, n + 1)
                    dve.wait_ge(taper_landed[n % 2], 16 * (n // 2 + 1))
                    if c:
                        dve.wait_ge(piece_sum, t // 2 + 1)
                    dve.tensor_tensor(taps[:, t, :], psum[:, 6 + n % 2, :], taper[:, n % 2, :], ALU.mult).then_inc(taps_ready, 1)

            def make_filter(c):
                for d in range(3):
                    n = 4 * c + d + 1
                    dve.wait_ge(piece_ready, n + 1)
                    if c:
                        dve.wait_ge(filt_stored[d], 16)
                    new, old = piece[:, n % 2], piece[:, (n - 1) % 2]
                    dve.scalar_tensor_tensor(filt[:, d, 0:2, :], old[:, 2:4, :], sign[:, 1:2], new[:, 0:2, :], ALU.mult, ALU.add)
                    dve.scalar_tensor_tensor(filt[:, d, 2:4, :], old[:, 0:2, :], sign[:, 0:1], new[:, 2:4, :], ALU.mult,
                                             ALU.add).then_inc(filt_ready, 1)

            def gain_pre(layer, i):
                dve.wait_ge(mod_ready, at["group"])
                for who in range(2):
                    ins = dve.scalar_tensor_tensor(gain_in[:, layer, i, who, :], mod[:, layer, 3 * i + SCALE, who, :], 1.0,
                                                   g_pre[:, layer, i, :], ALU.add, ALU.mult)
                ins.then_inc(dve_step, 1)

            def gain_post(layer, i, w):
                dve.wait_ge(mod_ready, at["group"])
                for who in range(2):
                    ins = dve.scalar_tensor_tensor(gain_out[:, layer, i, who, :], mod[:, layer, 3 * i + GATE, who, :], w,
                                                   g_post[:, layer, i, :], ALU.mult, ALU.mult)
                ins.then_inc(dve_step, 1)

            def hidden(layer):
                two_pi = 2.0 * math.pi
                c1 = 6.28125
                c2 = float((np.float32(two_pi - c1).view(np.uint32) & np.uint32(0xFFFFF000)).view(np.float32))
                c3 = two_pi - c1 - c2
                magic = 1.5 * 2 ** 23
                edge = float(np.nextafter(np.float32(math.pi), np.float32(0)))
                a, k = hid_t, hid[0:HID, 1, :]
                dve.wait_ge(hid_sum, layer + 1)
                seq(dve.tensor_scalar(a[:, :], psum[0:HID, 6:8, :].rearrange("p b c -> p (b c)"), fb[:, layer:layer + 1], fb[:, 3:4],
                                      ALU.add, ALU.mult))
                seq(dve.tensor_scalar(k, a[:, :], 1.0 / two_pi, magic, ALU.mult, ALU.add))
                seq(dve.tensor_scalar(k, k, magic, None, ALU.subtract))
                for c in (c1, c2, c3):
                    seq(dve.scalar_tensor_tensor(a[:, :], k, -c, a[:, :], ALU.mult, ALU.add))
                dve.tensor_scalar(a[:, :], a[:, :], -edge, edge, ALU.max, ALU.min).then_inc(hid_arg, 1)

            def gate_up(s, T):
                b0, p0, f0, g0 = s.first, at["p"], at["f"], at["group"]

                def step(i, last):
                    for j in range(2):
                        ahead(s, i, 2 * j + 2, last)
                        ahead(s, i, 2 * j + 3, last)
                        if s.mods and j == 1:
                            mod_copy(g0 + i)
                        bank = (p0 + 2 * j + 1) % 4
                        dve.wait_ge(block_done, RING + b0 + 4 * i + 2 * j + 2)
                        dve.wait_ge(silu_ready, f0 + 2 * i + j + 1)
                        ins = dve.tensor_tensor(prod[:, j, 0:T], psum[:, bank, 0:T], silu[:, j, 0:T], ALU.mult)
                        ins.then_inc(result_read, 2)
                        dve.wait_ge(act_hi_ready, f0 + 2 * i + j + 1)
                        dve.wait_ge(result_read, BANKS + p0 + 4 * i + 2 * j + 2)
                        fl = bass.ds(2 * i + j, 1)
                        dve.tensor_tensor(act_lo[:, fl, 0:T], prod[:, j:j + 1, 0:T], act_hi[:, fl, 0:T].bitcast(F32),
                                          ALU.subtract).then_inc(act_ready, 1)
                    if s.mods:
                        mod_finish(g0 + i, s.mods[0], s.mods[1] + i)
                stepped(dve, s.blocks // 4, step, s.layers, hidden)
                at["p"] += s.blocks
                at["f"] += s.blocks // 2
                if s.mods:
                    at["group"] += s.blocks // 4

            def add_square(n, T, d):
                dve.wait_ge(square_ready, n + 1)
                if d is not None and d == 0:
                    dve.tensor_copy(sumsq[:, 0:T], square[:, 0, 0:T]).then_inc(square_used, 1)
                    return
                dve.wait_ge(square_used, n)
                dve.tensor_tensor(sumsq[:, 0:T], sumsq[:, 0:T], square[:, d % 2, 0:T], ALU.add).then_inc(square_used, 1)

            def down(s, T, final):
                b0, p0, g0, n0 = s.first, at["p"], at["group"], KT * at["norm"]
                if final:
                    dve.memset(sumsq[:, 0:T], 0.0).then_inc(zeroed, 1)
                    at["z"] = at["z"] + 1
                    dve.wait_ge(zeroed, at["z"])

                def step(i, last):
                    for dd in range(2):
                        ahead(s, i, 2 * dd + 2, last)
                        ahead(s, i, 2 * dd + 3, last)
                        if s.mods and dd == 1:
                            mod_copy(g0 + i)
                        bank = DOWN_BANK[dd]
                        dve.wait_ge(block_done, RING + b0 + 4 * i + 2 * dd + 2)
                        dst = y[:, bass.ds(2 * i + dd, 1), 0:T]
                        src = psum[:, bank:bank + 1, 0:T]
                        if not final:
                            dve.tensor_copy(dst, src).then_inc(result_read, 1)
                        else:
                            ins = dve.tensor_tensor(dst, src, dst, ALU.add)
                            ins.then_inc(result_read, 1)
                            n = n0 + 2 * i + dd
                            dve.wait_ge(square_ready, n + 1)
                            dve.wait_ge(square_used, n)
                            dve.tensor_tensor(sumsq[:, 0:T], sumsq[:, 0:T], square[:, dd, 0:T],
                                              ALU.add).then_inc(square_used, 1)
                    if s.mods:
                        mod_finish(g0 + i, s.mods[0], s.mods[1] + i)
                stepped(dve, s.blocks // 4, step, s.layers, hidden)
                at["p"] += s.blocks // 2
                if s.mods:
                    at["group"] += s.blocks // 4

            def norm(T):
                n = at["norm"]
                nt = T // P
                dve.wait_ge(rms_ready, n + 1)
                dve.reciprocal(rinv[:, 0:nt], rms[:, 0:nt]).then_inc(rinv_ready, 1)
                dve.wait_ge(rinv_ready, n + 1)
                for t in range(nt):
                    ins = dve.tensor_scalar(rinv_wide[:, t, :], ones[:, :], rinv[:, t:t + 1], None, ALU.mult)
                ins.then_inc(wide_ready, 1)
                dve.wait_ge(rbc_ready, n + 1)
                at["norm"] += 1

            def adaln_in(src, T, hi, lo, rinv_all=None):
                c0 = KT * at["pre"]
                if rinv_all is None:
                    rinv_all = psum[:, RBC, 0:T]
                for d in range(KT + 1):
                    if d < KT:
                        dve.tensor_tensor(prod[:, d % 2, 0:T], src[:, d, 0:T], rinv_all, ALU.mult).then_inc(norm_ready, 1)
                    if d >= 1:
                        e = d - 1
                        dve.wait_ge(h_hi_ready, c0 + e + 1)
                        dve.tensor_tensor(lo[:, e, 0:T], full[:, e % 2, 0:T], hi[:, e, 0:T].bitcast(F32),
                                          ALU.subtract).then_inc(h_ready, 1)
                at["pre"] += 1

            def adaln_out(dst, T, layer, i, who, chain):
                n0 = KT * at["norm"]
                for d in range(KT + 1):
                    if d < KT:
                        dve.tensor_tensor(full[:, d % 2, 0:T], y[:, d, 0:T], psum[:, RBC, 0:T],
                                          ALU.mult).then_inc(dve_step, 1)
                        at["step"] += 1
                        dve.wait_ge(dve_step, at["step"])
                        dve.scalar_tensor_tensor(dst[:, d, 0:T], full[:, d % 2, 0:T],
                                                 gain_out[:, layer, i, who, d:d + 1], dst[:, d, 0:T],
                                                 ALU.mult, ALU.add).then_inc(x_ready, 1)
                    if d >= 1 and chain:
                        add_square(n0 + d - 1, T, d - 1)
                at["xr"] += KT

            def ffn(ss, T, layer, i, who, src, chain):
                if ss is not ffns[1]:
                    gain_pre(layer, i)
                    at["step"] += 1
                    dve.wait_ge(dve_step, at["step"])
                if ss not in ffns[0:2]:
                    norm(T)
                if ss is not ffns[1]:
                    adaln_in(src, T, h_hi, h_lo)
                gate_up(ss[0], T)
                if ss is ffns[1]:
                    norm(SEQ)
                    seq(dve.tensor_copy(kept_rinv[:, :], psum[:, RBC, :]))
                down(ss[1], T, False)
                gate_up(ss[2], T)
                down(ss[3], T, True)
                norm(T)
                if ss is ffns[0]:
                    dve.wait_ge(act_ready, at["f"])
                    adaln_in(cx, CTX, h_hi, h_lo, kept_rinv[:, 0:CTX])
                    mod_copy(at["group"])
                if ss is ffns[3]:
                    make_taps(0)
                gain_post(layer, i, 0.5)
                at["step"] += 1
                dve.wait_ge(dve_step, at["step"])
                adaln_out(src, T, layer, i, who, chain)
                if ss is ffns[0]:
                    mod_finish(at["group"], 0, 8)
                    at["group"] += 1

            def seq(ins):
                ins.then_inc(dve_step, 1)
                at["step"] += 1
                dve.wait_ge(dve_step, at["step"])

            for d in range(KT):
                add_square(d, CTX, d)
            norm(CTX)
            seq(dve.tensor_copy(kept_rinv[:, 0:CTX], psum[:, RBC, 0:CTX]))
            mod_copy(0)
            for d in range(KT):
                add_square(KT + d, SEQ, d)
            dve.wait_ge(loaded, 16 * LOADS)
            mod_finish(0, 0, 0)
            mod_copy(1)
            norm(SEQ)
            mod_finish(1, 0, 1)
            at["group"] += 2
            for b in range(2):
                split_lo(b, 0, 1024)
            ffn(ffns[0], SEQ, 0, 0, 0, x, True)

            ffn(ffns[1], CTX, 0, 0, 1, cx, True)

            def split_ahead(b):
                if b + 2 < total_blocks:
                    split_lo(b + 2, 0, cols_of(b + 2))

            def log_sigmoid():
                n = 2 * HEADS
                seq(dve.tensor_scalar(ls[:, 2, :], ret[:, :], -1.0, None, ALU.mult))
                dve.tensor_tensor(ls[:, 0, :], ret[:, :], ls[:, 2, :], ALU.max).then_inc(ls_in, 1)
                dve.wait_ge(ls_exp, 1)
                seq(dve.tensor_scalar(ls[:, 2, :], ls[:, 1, :], 2.0, None, ALU.add))
                seq(dve.reciprocal(ls[:, 3, :], ls[:, 2, :]))
                seq(dve.tensor_tensor(ls[:, 4, :], ls[:, 1, :], ls[:, 3, :], ALU.mult))
                seq(dve.tensor_tensor(ls[:, 5, :], ls[:, 4, :], ls[:, 4, :], ALU.mult))
                seq(dve.tensor_scalar(ls[:, 2, :], ls[:, 5, :], 1.0 / 19, None, ALU.mult))
                for k in range(8, 0, -1):
                    seq(dve.scalar_tensor_tensor(ls[:, 2, :], ls[:, 2, :], 1.0 / (2 * k + 1), ls[:, 5, :], ALU.add, ALU.mult))
                seq(dve.scalar_tensor_tensor(ls[:, 3, :], ls[:, 2, :], 1.0, ls[:, 4, :], ALU.add, ALU.mult))
                seq(dve.tensor_scalar(ls[:, 0, :], ret[:, :], 0.0, None, ALU.min))
                seq(dve.scalar_tensor_tensor(log_decay[:, :], ls[:, 3, :], -2.0, ls[:, 0, :], ALU.mult, ALU.add))
                seq(dve.tensor_scalar(log_decay[:, HEADS:n], log_decay[:, HEADS:n], -1.0, None, ALU.mult))

            def mixer_in():
                gain_pre(0, 1)
                at["step"] += 1
                dve.wait_ge(dve_step, at["step"])
                norm(CTX)
                adaln_in(cx, CTX, hc_hi, hc_lo)
                adaln_in(x, SEQ, h_hi, h_lo, kept_rinv[:, :])
                rotated = values = 0
                dve.wait_ge(padded, 2)
                dve.wait_ge(side_loaded, 16)

                def rotate(bank, tile):
                    nonlocal rotated
                    r = rotated % 2
                    if tile == RK[0]:
                        dve.wait_ge(side_loaded, 32)
                    dve.wait_ge(rot_ready, rotated + 1)
                    dve.tensor_tensor(prod[:, r, :], psum[:, bank, :], rope[:, 0, :], ALU.mult).then_inc(result_read, 1)
                    seq(dve.tensor_tensor(square[:, r, :], psum[:, 4 + r, :], rope[:, 1, :], ALU.mult))
                    at["p"] += 1
                    dve.wait_ge(result_read, BANKS + at["p"])
                    if tile in AQ or tile in RK:
                        dst = aq[:, tile, :] if tile in AQ else rk[:, tile - RK[0], 0:SEQ]
                        ins = dve.tensor_tensor(dst, prod[:, r, :], square[:, r, :], ALU.add)
                    elif tile in RQ:
                        for half in range(2):
                            rows = slice(HEAD * half, HEAD * half + HEAD)
                            ins = dve.tensor_tensor(rq[rows, 2 * (tile - RQ[0]) + half, :], prod[rows, r, :], square[rows, r, :], ALU.add)
                    else:
                        for g in range(2):
                            for half in range(2):
                                src, dst = slice(HEAD * g, HEAD * g + HEAD), slice(HEAD * half, HEAD * half + HEAD)
                                ins = dve.tensor_tensor(ak[dst, 2 * g + half, 0:SEQ], prod[src, r, :], square[src, r, :], ALU.add)
                    ins.then_inc(roped, 1)
                    rotated += 1

                for n, tile in enumerate(ORDER):
                    b = mix_in.first + n
                    split_ahead(b)
                    if tile == RQ[0]:
                        log_sigmoid()
                    dve.wait_ge(block_done, RING + b + 1)
                    bank = at["p"] % 4
                    if tile in VALUES:
                        if values:
                            dve.wait_ge(v_turned, values)
                        dve.tensor_copy(sumsq[:, :], psum[:, bank, :]).then_inc(result_read, 1)
                        dve.tensor_copy(prod[:, 1, 0:CTX], psum[:, (bank + 1) % 4, 0:CTX]).then_inc(result_read, 1)
                        at["p"] += 2
                        dve.wait_ge(result_read, BANKS + at["p"])
                        dve.sem_inc(v_copied, 1)
                        values += 1
                    elif tile in RG:
                        ins = dve.tensor_copy(rg[:, tile - RG[0], :], psum[:, bank, :])
                        ins.then_inc(result_read, 1)
                        at["p"] += 1
                    elif tile in WITH_CTX:
                        ctx_bank = (bank + 1) % 4
                        if tile in RK:
                            seq(dve.tensor_copy(rk[:, tile - RK[0], SEQ:ALL], psum[:, ctx_bank, 0:CTX]))
                        else:
                            for g in range(2):
                                for half in range(2):
                                    src, dst = slice(HEAD * g, HEAD * g + HEAD), slice(HEAD * half, HEAD * half + HEAD)
                                    ins = dve.tensor_copy(ak[dst, 2 * g + half, SEQ:ALL], psum[src, ctx_bank, 0:CTX])
                            seq(ins)
                        rotate(bank, tile)
                        dve.sem_inc(result_read, 1)
                        at["p"] += 1
                    else:
                        rotate(bank, tile)
                dve.wait_ge(result_read, BANKS + at["p"])
                dve.sem_inc(gate_ready, 1)

            def attention_retention():
                dve.wait_ge(side_loaded, 64)

                def take(u):
                    h, n, lo, hi, w = window(u)
                    own, m, i = w - CTX, (lo - n + 1) * P, u % 2
                    dve.wait_ge(scores_ready, u + 1)
                    if u >= 2:
                        dve.wait_ge(probs_turned, u - 1)
                    dve.scalar_tensor_tensor(probs[:, i, 0:own], psum[:, 2 * i, 0:own], QK_SCALE, mask[:, m:m + own], ALU.mult, ALU.add)
                    seq(dve.tensor_scalar(probs[:, i, own:w], psum[:, 2 * i + 1, 0:CTX], QK_SCALE, None, ALU.mult))
                    seq(dve.tensor_reduce(stats[:, i, 0:1], probs[:, i, 0:w], AX.X, ALU.max))
                    dve.tensor_scalar(stats[:, i, 1:2], stats[:, i, 0:1], sink[:, h:h + 1], -1.0, ALU.max,
                                      ALU.mult).then_inc(scores_read, 1)

                def normalize(u):
                    w, i = window(u)[4], u % 2
                    dve.wait_ge(exp_ready, u + 1)
                    seq(dve.tensor_tensor(stats[:, i, 4:5], stats[:, i, 2:3], stats[:, i, 3:4], ALU.add))
                    dve.reciprocal(stats[:, i, 5:6], stats[:, i, 4:5]).then_inc(rsum_ready, 1)

                def att_out(t):
                    dve.wait_ge(att_hi_ready, t + 1)
                    dve.tensor_tensor(h_lo[:, t, :], psum[:, 4, :], h_hi[:, t, :].bitcast(F32),
                                      ALU.subtract).then_inc(att_out_ready, 1)

                def corner_of(h):
                    d = dist[:, ZERO:ZERO + P]
                    seq(dve.tensor_scalar(corner[:, :], d, log_decay[:, h:h + 1], None, ALU.mult))
                    dve.scalar_tensor_tensor(corner[:, :], d, log_decay[:, HEADS + h:HEADS + h + 1], corner[:, :], ALU.mult,
                                             ALU.min).then_inc(arg_ready, 1)

                def weigh(i):
                    h, j = divmod(i, KEY_TILES)
                    dve.wait_ge(ret_scores, i + 1)
                    if i >= 3:
                        dve.wait_ge(ret_done, i - 2)
                    if j == 0:
                        dve.wait_ge(table_ready, 2 * h + 1)
                        if h + 1 < HEADS:
                            corner_of(h + 1)
                    if j == 4:
                        dve.wait_ge(table_ready, 2 * h + 2)
                    w = decay[:, ZERO - j * P:ZERO - j * P + SEQ] if j < 4 else decay_ctx[:, j - 4, :]
                    bank = 5 + (i + sums_before(step_of(i))) % 2
                    dve.scalar_tensor_tensor(weighed[i % 3], psum[:, bank, :], QK_SCALE, w, ALU.mult, ALU.mult).then_inc(att_ready, 1)

                def invert(t, part):
                    dve.wait_ge(orms_ready, t + 1)
                    part = slice(part * P, part * P + P)
                    dve.reciprocal(full[:, 0, part], full[:, 1, part]).then_inc(dve_step, 1)
                    at["step"] += 1

                def finish(t):
                    dve.wait_ge(dve_step, at["step"])
                    seq(dve.tensor_tensor(prod[:, 0, :], prod[:, 0, :], full[:, 0, :], ALU.mult))
                    dve.tensor_tensor(full[:, 0, :], prod[:, 0, :], silu_g[:, t, :], ALU.mult).then_inc(oval_ready, 1)

                def ret_out(t):
                    dve.wait_ge(ret_hi_ready, t + 1)
                    dve.tensor_tensor(h_lo[:, 4 + t, :], full[:, 0, :], h_hi[:, 4 + t, :].bitcast(F32),
                                      ALU.subtract).then_inc(ret_out_ready, 1)

                dve.wait_ge(gate_ready, 2)
                corner_of(0)
                for s in range(MIX_STEPS):
                    if s >= 10 and (s - 10) % 8 == 0 and s <= UNITS + 2:
                        att_out((s - 10) // 8)
                    if 1 <= s <= UNITS:
                        normalize(s - 1)
                    if s < UNITS:
                        take(s)
                    if s - INVERTED - 3 in PAIR_END:
                        ret_out(PAIR_END.index(s - INVERTED - 3))
                    for i in items_of(s):
                        if i < ITEMS:
                            weigh(i)
                    for part in range(4):
                        if s - 2 - part in PAIR_END:
                            invert(PAIR_END.index(s - 2 - part), part)
                    if s - 2 - INVERTED in PAIR_END:
                        finish(PAIR_END.index(s - 2 - INVERTED))

            def project(s):
                n0, b0 = KT * at["norm"], s.first
                seq(dve.memset(sumsq[:, :], 0.0))
                for d in range(KT):
                    split_ahead(b0 + d)
                    dve.wait_ge(block_done, RING + b0 + d + 1)
                    dve.tensor_copy(y[:, d, :], psum[:, at["p"] % 4, :]).then_inc(result_read, 1)
                    at["p"] += 1
                    dve.wait_ge(square_ready, n0 + d + 1)
                    dve.wait_ge(square_used, n0 + d)
                    dve.tensor_tensor(sumsq[:, :], sumsq[:, :], square[:, d % 2, :], ALU.add).then_inc(square_used, 1)

            def mixer_post(layer):
                norm(SEQ)
                gain_post(layer, 1, 1.0)
                at["step"] += 1
                dve.wait_ge(dve_step, at["step"])
                adaln_out(x, SEQ, layer, 1, 0, True)

            mixer_in()
            attention_retention()
            project(mix_out)
            mixer_post(0)

            ffn(ffns[2], SEQ, 0, 2, 0, x, True)
            ffn(ffns[3], SEQ, 1, 0, 0, x, True)

            def hyena():
                gain_pre(1, 1)
                at["step"] += 1
                dve.wait_ge(dve_step, at["step"])
                norm(SEQ)
                for d in range(3):
                    dve.wait_ge(filt_stored[d], 32)
                adaln_in(x, SEQ, h_hi, h_lo)
                for n in range(24):
                    b = hy_in.first + n
                    if n < 22:
                        split_ahead(b)
                    d, kind = divmod(n, 3)
                    col = (8, 16, 0)[kind] + d
                    dst = x0[:, d, :] if kind == 2 else short[:, kind, :]
                    dve.wait_ge(mid_ready, n + 1)
                    dve.scalar_tensor_tensor(dst, zp[:, n % 2, 0:SEQ], hy_cols[:, 1, col:col + 1], dst, ALU.mult, ALU.add).then_inc(result_read, 1)
                    at["p"] += 1
                    dve.wait_ge(result_read, BANKS + at["p"])
                    dve.scalar_tensor_tensor(dst, zp[:, n % 2, 2:SEQ + 2], hy_cols[:, 3, col:col + 1], dst, ALU.mult, ALU.add).then_inc(conv_done, 1)
                    if kind == 1:
                        dve.wait_ge(conv_done, n + 1)
                        dve.tensor_tensor(u_t[:, d, :], short[:, 0, :], short[:, 1, :], ALU.mult).then_inc(u_t_ready, 1)

                def gate(n):
                    dve.wait_ge(back_ready, n + 1)
                    if n >= 2:
                        dve.wait_ge(g_ready, n - 1)
                    seq(dve.scalar_tensor_tensor(square[:, n % 2, :], u_t[:, n, :], hy_bias[:, n:n + 1], psum[:, 4 + n % 2, :],
                                                 ALU.mult, ALU.add))
                    dve.tensor_tensor(u_t[:, n, :], square[:, n % 2, :], x0[:, n, :], ALU.mult).then_inc(g_ready, 1)

                def split_g(tiles):
                    for d in tiles:
                        dve.wait_ge(g_hi_ready, d + 1)
                        dve.tensor_tensor(h_lo[:, d, :], u_t[:, d, :], h_hi[:, d, :].bitcast(F32), ALU.subtract).then_inc(g_split, 1)

                for c in range(2):
                    dve.wait_ge(filt_loaded, 16 * (c + 1))
                    dve.wait_ge(uf_ready, 8 * c + 8)
                    if c:
                        dve.wait_ge(yf_pool_ready, 1)
                    for n, (i, part) in enumerate(((0, 0), (0, 1), (1, 0))):
                        at["step"] = products(dve, dve_step, at["step"], c, i, part, term[:, 0, :], term[:, 1, :], yf_ready,
                                              3 * c + n)
                    if c:
                        split_g(range(4))
                        split_lo(hy_out.first, 0, 1024)
                        split_lo(hy_out.first + 1, 0, 1024)
                    for t in range(4):
                        gate(4 * c + t)
                split_g(range(4, KT))

            make_filter(0)
            make_taps(1)
            make_filter(1)
            hyena()
            project(hy_out)
            mixer_post(1)
            ffn(ffns[4], SEQ, 1, 2, 0, x, False)

        @block.gpsimd
        def _(pool):
            def load_mods(layer):
                with pool.Fori(0, NMOD) as v:
                    for k in range(KT):
                        pool.wait_ge(mod_used, KT * (NMOD * layer + v) + k + 1)
                        pool.dma_start(mod_raw[:, k % RING, :], io["w_mod"][layer, v, k]).then_inc(mod_landed[k % RING], 16)

            load_mods(0)
            pool.wait_ge(x_ready, 16)
            pool.dma_start(rope[:], io["rope"][:, 0:2]).then_inc(side_loaded, 16)
            pool.memset(ak[:], 0.0).then_inc(padded, 1)
            pool.memset(rq[:], 0.0).then_inc(padded, 1)
            pool.wait_ge(roped, 5)
            pool.dma_start(rope[:], io["rope"][:, 2:4]).then_inc(side_loaded, 16)
            pool.wait_ge(block_done, RING + mix_in.first + ORDER.index(RK[-1]) + 1)
            pool.dma_start(mask[:], io["mask"]).then_inc(side_loaded, 16)
            pool.dma_start(dist[:], io["dist"]).then_inc(side_loaded, 16)
            for h in range(HEADS):
                pool.wait_ge(decay_exp, h + 1)
                pool.tensor_tensor(decay[:, ZERO:ZERO + P], decay[:, ZERO:ZERO + P], ident[:, :], ALU.add).then_inc(table_ready, 1)
                if h:
                    pool.wait_ge(att_ready, KEY_TILES * h)
                for c in range(2):
                    fwd, bwd = ZERO + CTX - c * P, ZERO - SEQ - c * P
                    ins = pool.tensor_tensor(decay_ctx[:, c, :], decay[:, fwd:fwd + SEQ], decay[:, bwd:bwd + SEQ], ALU.add)
                ins.then_inc(table_ready, 1)
            pool.wait_ge(x_ready, 24)
            load_mods(1)
            pool.wait_ge(mod_used, RING + 2 * NMOD * KT)
            for dst, src in ((pos[:], io["pos"]), (f0[:], io["hy_f0"]), (f12[:, 0, :], io["hy_f1"]), (f12[:, 1, :], io["hy_f2"]),
                             (fb[:], io["hy_fb"])):
                pool.dma_start(dst, src).then_inc(side_loaded, 16)
            pool.wait_ge(block_done, RING + hy_in.first)
            pool.dma_start(f3[0:HID, :], io["hy_f3"]).then_inc(side_loaded, 16)
            pool.dma_start(dft_f[:], io["dft"]).then_inc(side_loaded, 16)
            pool.memset(f3[HID:P, :], 0.0).then_inc(padded, 1)
            pool.memset(hid[HID:P, 0, :], 0.0).then_inc(padded, 1)
            def load_tapers(first, last):
                for n in range(first, last):
                    c, t = divmod(n, POS_TILES)
                    if n >= 2:
                        pool.wait_ge(taps_ready, n - 1)
                    pool.dma_start(taper[:, n % 2, :], io["decay"][t, :, c * 512:c * 512 + 512]).then_inc(taper_landed[n % 2], 16)

            def store_filter(c):
                for d in range(3):
                    pool.wait_ge(filt_ready, 3 * c + d + 1)
                    pool.dma_start(filt_dram[c][:, d], filt[:, d]).then_inc(filt_stored[d], 16)

            load_tapers(0, POS_TILES + 2)
            store_filter(0)
            load_tapers(POS_TILES + 2, 2 * POS_TILES)
            store_filter(1)
            pool.dma_start(hy_cols[:, 0, :], io["hy_b_in"]).then_inc(side_loaded, 16)
            pool.dma_start(hy_cols[:, 1:4, :], io["hy_short_w"]).then_inc(side_loaded, 16)
            pool.dma_start(hy_cols[:, 4, :], io["hy_short_b"]).then_inc(side_loaded, 16)
            pool.dma_start(hy_bias[:, :], io["hy_bias"]).then_inc(side_loaded, 16)
            pool.memset(zp[:], 0.0).then_inc(padded, 1)
            pool.wait_ge(u_t_ready, KT)
            pool.wait_ge(conv_done, 24)
            pool.dma_start(dft[:], io["dft"]).then_inc(side_loaded, 16)
            pool.dma_start(idft[:], io["idft"]).then_inc(side_loaded, 16)
            step = 0
            for c in range(2):
                pool.wait_ge(block_done, RING + hy_in.first + 24)
                if c:
                    pool.wait_ge(yf_ready, 3)
                    pool.wait_ge(yf_pool_ready, 1)
                for d in range(3):
                    pool.wait_ge(filt_stored[d], 32)
                pool.dma_start(filt[:], filt_dram[c]).then_inc(filt_loaded, 16)
                pool.wait_ge(filt_loaded, 16 * (c + 1))
                pool.wait_ge(uf_ready, 8 * c + 8)
                step = products(pool, pool_step, step, c, 1, 1, prod[:].rearrange("p a c -> p (a c)"),
                                full[:].rearrange("p a c -> p (a c)"), yf_pool_ready, c)

    return nc


def constants():
    t = {}
    t["ident"] = np.eye(P, dtype=np.float32)
    half = HEAD // 2
    rot = np.zeros((P, P), np.float32)
    for m in range(P):
        base, r = m // HEAD * HEAD, m % HEAD
        if r < half:
            rot[base + r + half, m] = -1.0
        else:
            rot[base + r - half, m] = 1.0
    t["rot"] = rot
    grid_w = 64
    pos = np.arange(SEQ)
    row, col = (pos // grid_w).astype(np.float32), (pos % grid_w).astype(np.float32)
    nf = HEAD // 4
    inv = (np.float32(10000.0) ** (-np.arange(nf, dtype=np.float32) / nf)).astype(np.float32)
    ang_a = np.concatenate([row[:, None] * inv, col[:, None] * inv], -1).astype(np.float32)
    inv_r = (np.float32(10000.0) ** (-np.linspace(0.0, 1.0, half, dtype=np.float32))).astype(np.float32)
    ang_r = (pos.astype(np.float32)[:, None] * inv_r).astype(np.float32)
    rope = np.zeros((P, 4, SEQ), np.float32)
    for n, ang in enumerate((ang_a, ang_r)):
        rope[:, 2 * n] = np.tile(np.cos(ang).T, (4, 1))
        rope[:, 2 * n + 1] = np.tile(np.sin(ang).T, (4, 1))
    t["rope"] = rope
    q, k = np.arange(P)[:, None], np.arange(3 * P)[None]
    t["mask"] = np.where(np.abs(k - P - q) <= P, 0.0, NEG).astype(np.float32)
    dist = np.arange(G_W)[None] + G_LOW - 3 * P - np.arange(P)[:, None]
    t["dist"] = dist.astype(np.float32)
    two = np.zeros((P, P), np.float32)
    two[:HEAD, :HEAD] = 1.0
    two[HEAD:, HEAD:] = 1.0
    t["head_ones"] = two
    lag = np.arange(-SEQ, SEQ)
    at = np.abs(lag)
    L = SEQ
    bands = (EMB - 1) // 2
    tt = np.append(np.linspace(0.0, 1.0, L, dtype=np.float32), np.float32(1.0))[at]
    w = np.float32(2.0 * math.pi) * at.astype(np.float32) / np.float32(L)
    f = np.linspace(1e-4, bands - 1, bands, dtype=np.float32)
    fw = (f[:, None] * w[None]).astype(np.float32)
    t["pos"] = np.concatenate([tt[None], np.cos(fw), -np.sin(fw)], 0).astype(np.float32)
    lo, hi = math.log(1e-2) / 1.5, math.log(1e-2) / 0.3
    deltas = np.abs(np.linspace(lo, hi, D, dtype=np.float32))
    t["decay"] = np.ascontiguousarray(np.exp(-tt[:, None] * deltas[None]).astype(np.float32).reshape(POS_TILES, P, D))
    n = np.arange(HB)[:, None].astype(np.float64)
    th = math.pi * (2 * np.arange(HB)[None] + 1) / (2 * HB)
    fwd = np.concatenate([np.cos(n * th), -np.sin(n * th)], 1)
    t["dft"] = np.ascontiguousarray(fwd.reshape(2, P, 4, P).transpose(1, 0, 2, 3)).astype(np.float32)
    back = np.concatenate([np.cos(n * th).T, -np.sin(n * th).T], 0) / HB
    t["idft"] = np.ascontiguousarray(back.reshape(4, P, HB).transpose(1, 0, 2)).astype(np.float32)
    sign = np.where(np.arange(P) % 2 == 0, 1.0, -1.0)
    t["sign"] = np.stack([sign, -sign], 1).astype(np.float32)
    return t


def tiles(w):
    K, M = w.shape
    return w.reshape(K // P, P, M // P, P).transpose(2, 1, 0, 3).reshape(M // P, P, K)


def columns(v):
    return np.moveaxis(v.reshape(v.shape[:-1] + (v.shape[-1] // P, P)), -1, 0)


def layout(inp):
    a = {k: np.asarray(v) for k, v in inp.items()}
    o = {}
    o["x"] = a["x"][0].reshape(SEQ, KT, P).transpose(2, 1, 0)
    o["ctx"] = a["ctx"][0].reshape(CTX, KT, P).transpose(2, 1, 0)
    o["c_cols"] = np.stack([columns(a["c"][0]), columns(a["c_ctx"])], -1)
    o["w_mod"] = a["w_mod"].reshape(2, KT, P, NMOD, D).transpose(0, 3, 1, 2, 4)
    o["b_mod"] = columns(a["b_mod"].reshape(2, NMOD, D))
    o["g_pre"] = columns(a["norm_pre"])
    o["g_post"] = columns(a["norm_post"])
    gu, da, db = [], [], []
    for l in range(2):
        for j in range(2):
            pair = np.stack([tiles(a["ffn_gate"][l, j]), tiles(a["ffn_up"][l, j])], 1)
            gu.append(pair.reshape(2 * FT, P, D))
            down = a["ffn_down"][l, j].reshape(FT, P, KT, P).transpose(2, 1, 0, 3)
            n = HALF_TILES[0]
            for out, part, per in ((da, down[:, :, :n], n // 2), (db, down[:, :, n:], (FT - n) // 2)):
                out.append(part.reshape(KT, P, 2, per, P).transpose(0, 2, 1, 3, 4).reshape(2 * KT, P, per * P))
    o["gate_up"], o["down_a"], o["down_b"] = np.stack(gu), np.stack(da), np.stack(db)
    o["mix_in"] = tiles(a["mix_w_in"][0])[ORDER]
    o["mix_out"] = tiles(a["mix_w_out"][0])
    o["hy_in"] = tiles(a["hy_w_in"][0])[[t * KT + d for d in range(KT) for t in (1, 2, 0)]]
    o["hy_out"] = tiles(a["hy_w_out"][0])
    o["sink"] = np.broadcast_to(a["attn_sink"][0][None], (P, HEADS))
    o["ret"] = np.broadcast_to(a["ret_decay"][0].reshape(1, 2 * HEADS), (P, 2 * HEADS))
    o["hy_b_in"] = columns(a["hy_b_in"][0])
    o["hy_short_w"] = columns(a["hy_short_w"][0])
    o["hy_short_b"] = columns(a["hy_short_b"][0])
    o["hy_bias"] = columns(a["hy_bias"][0])
    o["hy_f0"], o["hy_f1"], o["hy_f2"], o["hy_f3"] = a["hy_f0"][0], a["hy_f1"][0], a["hy_f2"][0], a["hy_f3"][0]
    o["hy_fb"] = np.stack([a["hy_fb0"][0], a["hy_fb1"][0], a["hy_fb2"][0], a["hy_freq"][0]], -1)
    o.update(constants())
    return {k: np.ascontiguousarray(v) for k, v in o.items()}


def kernel(**inputs):
    import concourse.bacc as bacc
    from concourse.bass_utils import run_bass_kernel_spmd

    nc = bacc.Bacc("TRN2", target_bir_lowering=False, num_devices=1)
    arrays = layout(inputs)
    io = {k: nc.dram_tensor(f"in_{k}", v.shape, mybir.dt.from_np(v.dtype), kind="ExternalInput").ap()
          for k, v in arrays.items()}
    io["out"] = nc.dram_tensor("out", (P, KT, SEQ), F32, kind="ExternalOutput").ap()
    build(nc, io)
    r = run_bass_kernel_spmd(nc, [{f"in_{k}": v for k, v in arrays.items()}], core_ids=[0])
    got = r.results[0]["out"]
    return np.ascontiguousarray(got.transpose(2, 1, 0).reshape(1, SEQ, D))
```
